# Optimizing a Trainium2 kernel written in Bass

```python
import jax, jax.numpy as jnp
from jax import lax
import numpy as np

D_MODEL = 1024
BATCH = 1
SEQ = 256
DEPTH = 2

N_A_LAYERS = DEPTH // 2
N_B_LAYERS = DEPTH - N_A_LAYERS
MAIN_W = 3 * D_MODEL // 4
MEM_W = D_MODEL // 4
MIX_W = MAIN_W + MEM_W
GLA_HEADS = 4
GLA_DK = MAIN_W // 2
GLA_DV = MAIN_W
GLA_DK_HEAD = GLA_DK // GLA_HEADS
GLA_DV_HEAD = GLA_DV // GLA_HEADS
GLA_GATE_RANK = 16
GLA_GATE_TEMP = 16.0
GLA_CHUNK = 64
FOX_HEADS = 6
FOX_HEAD_DIM = MAIN_W // FOX_HEADS
FOX_BLOCK_Q = 128
FOX_FGATE_BIAS_INIT = 3.0
MEM_HEADS = 4
MEM_HEAD_DIM = MEM_W // MEM_HEADS
MEM_LEN = 256
D_FF = 256 * ((8 * D_MODEL // 3 + 255) // 256)
EPS = 1e-6
A_IN_W = 2 * GLA_DK + 2 * GLA_DV + GLA_GATE_RANK + MEM_W
B_IN_W = MAIN_W + MEM_W

kernel_name = "yoco_gla_fox_macaron_memory"

def rmsnorm(x, g):
    xf = x.astype(jnp.float32)
    y = xf * lax.rsqrt(jnp.mean(xf * xf, axis=-1, keepdims=True) + EPS)
    return (y * g.astype(jnp.float32)).astype(x.dtype)

def split_heads(t, n):
    b, s, w = t.shape
    return t.reshape(b, s, n, w // n).transpose(0, 2, 1, 3)

def merge_heads(t):
    b, n, s, d = t.shape
    return t.transpose(0, 2, 1, 3).reshape(b, s, n * d)

def swiglu_half_step(h, g, w_in, w_out):
    u = rmsnorm(h, g) @ w_in
    a, c = jnp.split(u, 2, axis=-1)
    return h + 0.5 * ((jax.nn.silu(a) * c) @ w_out)

def memory_attention(q_mem, mem_n, w_mem_kv):
    k, v = jnp.split(mem_n @ w_mem_kv, 2, axis=-1)
    q = split_heads(q_mem, MEM_HEADS)
    k = split_heads(k, MEM_HEADS)
    v = split_heads(v, MEM_HEADS)
    logits = jnp.einsum('bhqd,bhkd->bhqk', q, k).astype(jnp.float32) * (MEM_HEAD_DIM ** -0.5)
    p = jax.nn.softmax(logits, axis=-1).astype(v.dtype)
    return merge_heads(jnp.einsum('bhqk,bhkd->bhqd', p, v))

def gla_chunked(q, k, v, log_a):
    b, nh, s, dk = q.shape
    dv = v.shape[-1]
    nc = s // GLA_CHUNK

    def chunks(t):
        return t.astype(jnp.float32).reshape(b, nh, nc, GLA_CHUNK, t.shape[-1]).transpose(2, 0, 1, 3, 4)

    causal = jnp.tril(jnp.ones((GLA_CHUNK, GLA_CHUNK), dtype=bool))[:, :, None]

    def step(state, inp):
        qc, kc, vc, gc = inp
        cum = jnp.cumsum(gc, axis=2)
        o_inter = jnp.einsum('bhid,bhde->bhie', qc * jnp.exp(cum), state)
        diff = cum[:, :, :, None, :] - cum[:, :, None, :, :]
        decay = jnp.exp(jnp.where(causal, diff, -jnp.inf))
        scores = jnp.einsum('bhid,bhjd,bhijd->bhij', qc, kc, decay)
        o_intra = jnp.einsum('bhij,bhje->bhie', scores, vc)
        last = cum[:, :, -1:, :]
        k_dec = kc * jnp.exp(last - cum)
        state = jnp.exp(last[:, :, 0, :])[..., None] * state + jnp.einsum('bhjd,bhje->bhde', k_dec, vc)
        return state, o_inter + o_intra

    state0 = jnp.zeros((b, nh, dk, dv), jnp.float32)
    _, out = lax.scan(step, state0, (chunks(q), chunks(k), chunks(v), chunks(log_a)))
    return out.transpose(1, 2, 0, 3, 4).reshape(b, nh, s, dv)

def fox_attention(q, k, v, dcum):
    b, nh, s, dh = q.shape
    nb = s // FOX_BLOCK_Q
    qb = q.reshape(b, nh, nb, FOX_BLOCK_Q, dh).transpose(2, 0, 1, 3, 4)
    db = dcum.reshape(b, nh, nb, FOX_BLOCK_Q).transpose(2, 0, 1, 3)
    kpos = jnp.arange(s)
    scale = dh ** -0.5

    def block(args):
        i, qi, di = args
        logits = jnp.einsum('bhqd,bhkd->bhqk', qi, k).astype(jnp.float32) * scale
        logits = logits + di[..., :, None] - dcum[:, :, None, :]
        qpos = i * FOX_BLOCK_Q + jnp.arange(FOX_BLOCK_Q)
        logits = jnp.where(kpos[None, :] <= qpos[:, None], logits, -jnp.inf)
        p = jax.nn.softmax(logits, axis=-1).astype(v.dtype)
        return jnp.einsum('bhqk,bhkd->bhqd', p, v)

    out = lax.map(block, (jnp.arange(nb), qb, db))
    return out.transpose(1, 2, 0, 3, 4).reshape(b, nh, s, dh)

def gla_mixer(xn, mem_n, w_in, w_gate_up, b_gate, g_head, w_mem_kv, w_out):
    proj = xn @ w_in
    o1 = GLA_DK
    o2 = o1 + GLA_DK
    o3 = o2 + GLA_DV
    o4 = o3 + GLA_DV
    o5 = o4 + GLA_GATE_RANK
    q, k, v, r, g_low, q_mem = (proj[..., :o1], proj[..., o1:o2], proj[..., o2:o3],
                                proj[..., o3:o4], proj[..., o4:o5], proj[..., o5:])
    log_a = jax.nn.log_sigmoid((g_low @ w_gate_up + b_gate).astype(jnp.float32)) / GLA_GATE_TEMP
    o = gla_chunked(split_heads(q * (GLA_DK_HEAD ** -0.5), GLA_HEADS), split_heads(k, GLA_HEADS),
                    split_heads(v, GLA_HEADS), split_heads(log_a, GLA_HEADS))
    o = rmsnorm(o, g_head).astype(xn.dtype)
    o_main = merge_heads(o) * jax.nn.silu(r)
    o_mem = memory_attention(q_mem, mem_n, w_mem_kv)
    return jnp.concatenate([o_main, o_mem], axis=-1) @ w_out

def fox_mixer(xn, mem_n, w_in, k_sh, v_sh, dcum_sh, w_mem_kv, w_out):
    proj = xn @ w_in
    q, q_mem = proj[..., :MAIN_W], proj[..., MAIN_W:]
    o_main = merge_heads(fox_attention(split_heads(q, FOX_HEADS), k_sh, v_sh, dcum_sh))
    o_mem = memory_attention(q_mem, mem_n, w_mem_kv)
    return jnp.concatenate([o_main, o_mem], axis=-1) @ w_out

def setup_inputs(seed: int = 0) -> dict:
    key = jax.random.key(seed)
    ks = jax.random.split(key, 20)

    def dense(k, shape, fan_in, scale=1.0):
        return jax.random.normal(k, shape, jnp.float32) * (scale * fan_in ** -0.5)

    def gain(k, shape):
        return 1.0 + 0.02 * jax.random.normal(k, shape, jnp.float32)

    return {
        "x": jax.random.normal(ks[0], (BATCH, SEQ, D_MODEL), jnp.float32),
        "mem": jax.random.normal(ks[1], (BATCH, MEM_LEN, D_MODEL), jnp.float32),
        "norm_ffn": gain(ks[2], (DEPTH, 2, D_MODEL)),
        "w_ffn_in": dense(ks[3], (DEPTH, 2, D_MODEL, 2 * D_FF), D_MODEL),
        "w_ffn_out": dense(ks[4], (DEPTH, 2, D_FF, D_MODEL), D_FF, 0.5),
        "norm_mix": gain(ks[5], (DEPTH, D_MODEL)),
        "norm_mem": gain(ks[6], (DEPTH, D_MODEL)),
        "w_mem_kv": dense(ks[7], (DEPTH, D_MODEL, 2 * MEM_W), D_MODEL),
        "w_out": dense(ks[8], (DEPTH, MIX_W, D_MODEL), MIX_W, 0.5),
        "w_in_a": dense(ks[9], (N_A_LAYERS, D_MODEL, A_IN_W), D_MODEL),
        "w_gate_up": dense(ks[10], (N_A_LAYERS, GLA_GATE_RANK, GLA_DK), GLA_GATE_RANK),
        "b_gate": 0.1 * jax.random.normal(ks[11], (N_A_LAYERS, GLA_DK), jnp.float32),
        "norm_gla_head": gain(ks[12], (N_A_LAYERS, GLA_DV_HEAD)),
        "w_in_b": dense(ks[13], (N_B_LAYERS, D_MODEL, B_IN_W), D_MODEL),
        "norm_shared": gain(ks[14], (D_MODEL,)),
        "w_kv_shared": dense(ks[15], (D_MODEL, 2 * MAIN_W), D_MODEL),
        "w_fgate": dense(ks[16], (D_MODEL, FOX_HEADS), D_MODEL),
        "b_fgate": FOX_FGATE_BIAS_INIT + 0.1 * jax.random.normal(ks[17], (FOX_HEADS,), jnp.float32),
        "norm_final": gain(ks[18], (D_MODEL,)),
    }

def reference(x, mem, norm_ffn, w_ffn_in, w_ffn_out, norm_mix, norm_mem, w_mem_kv, w_out,
              w_in_a, w_gate_up, b_gate, norm_gla_head, w_in_b, norm_shared, w_kv_shared,
              w_fgate, b_fgate, norm_final):
    h = x
    k_sh = v_sh = dcum_sh = None
    for l in range(DEPTH):
        if l == N_A_LAYERS:
            hs = rmsnorm(h, norm_shared)
            k_all, v_all = jnp.split(hs @ w_kv_shared, 2, axis=-1)
            k_sh = split_heads(k_all, FOX_HEADS)
            v_sh = split_heads(v_all, FOX_HEADS)
            log_f = jax.nn.log_sigmoid((hs @ w_fgate + b_fgate).astype(jnp.float32))
            dcum_sh = jnp.cumsum(log_f, axis=1).transpose(0, 2, 1)
        h = swiglu_half_step(h, norm_ffn[l, 0], w_ffn_in[l, 0], w_ffn_out[l, 0])
        xn = rmsnorm(h, norm_mix[l])
        mem_n = rmsnorm(mem, norm_mem[l])
        if l < N_A_LAYERS:
            mixed = gla_mixer(xn, mem_n, w_in_a[l], w_gate_up[l], b_gate[l], norm_gla_head[l],
                              w_mem_kv[l], w_out[l])
        else:
            j = l - N_A_LAYERS
            mixed = fox_mixer(xn, mem_n, w_in_b[j], k_sh, v_sh, dcum_sh, w_mem_kv[l], w_out[l])
        h = h + mixed
        h = swiglu_half_step(h, norm_ffn[l, 1], w_ffn_in[l, 1], w_ffn_out[l, 1])
    return rmsnorm(h, norm_final)


_drawn_inputs = setup_inputs


def setup_inputs(seed=0):
    import zlib

    import numpy as np

    out = dict(_drawn_inputs(seed))
    spreads = {}
    factors = {'norm_ffn': 6.626,
     'norm_mix': 4.859,
     'norm_mem': 8.0,
     'b_gate': 5.197,
     'norm_gla_head': 8.0,
     'norm_shared': 22.591,
     'w_fgate': 3.518,
     'b_fgate': 64.0,
     'norm_final': 8.435}
    for name, (base, spread) in spreads.items():
        noise = np.random.default_rng([zlib.crc32(name.encode()), seed]).standard_normal(out[name].shape)
        drawn = base * np.exp(spread * noise) if base else spread * noise
        out[name] = __import__('jax').numpy.asarray(drawn.astype(out[name].dtype))
    for name, factor in factors.items():
        out[name] = (out[name] * factor).astype(out[name].dtype)
    return out
```

```python
from contextlib import ExitStack

import numpy as np

import concourse.bass as bass
from concourse import mybir

F32 = mybir.dt.float32
F32R = mybir.dt.float32r
U8 = mybir.dt.uint8
ALU = mybir.AluOpType
ACT = mybir.ActivationFunctionType
AX_X = mybir.AxisListType.X

P = 128
T = 2
D = 1024
KT = D // P
FF = 2816
STEPS = FF // 256
MAIN = 768
MEMW = 256
A_IN = 2576
GH, DK, DV = 4, 96, 192
RANK = 16
FH, FD = 6, 128
MH, MD = 4, 64
OUT_ORDER = (0, 2, 4, 6)
MEM_AT = [0, 2, 1, 3]
EPS = 1e-6
NLEV = 8
MASKED = -1.0e30
WORK = 16160
RING = 3

A_CHUNKS = [(2304, 272), (0, 512), (512, 512), (1024, 512), (1536, 512), (2048, 256)]

FFN_UNITS = 3 * STEPS
S_FFN0 = 0
S_MK0 = S_FFN0 + FFN_UNITS
S_PA = [S_MK0 + 2, S_MK0 + 4, S_MK0 + 6] + [S_MK0 + 10 + 2 * c for c in range(3)]
S_MK1 = S_PA[2] + 2
S_WO0 = S_PA[-1] + 2
S_FFN1 = S_WO0 + 4
S_FFN2 = S_FFN1 + FFN_UNITS
S_KV = [S_FFN2 + FFN_UNITS, S_FFN2 + FFN_UNITS + 2, S_FFN2 + FFN_UNITS + 9]
S_FG = S_KV[1] + 2
S_PB = S_FG + 1
S_WO1 = S_KV[2] + 2
S_FFN3 = S_WO1 + 4
S_END = S_FFN3 + FFN_UNITS
S_FFN = [S_FFN0, S_FFN1, S_FFN2, S_FFN3]
S_MK = [S_MK0, S_MK1]
S_WO = [S_WO0, S_WO1]

X, Y = 0, 1
NORMS = [("x", 0, X), ("mem", 6, Y), ("h", 4, X), ("mem", 7, Y), ("h", 1, X),
         ("h", 2, X), ("h", 8, Y), ("h", 5, X), ("h", 3, X)]
ST_X, ST_MEM, ST_H = 0, 1, 2


def shape_constants():
    i = np.arange(P)
    ident = np.eye(P, dtype=np.float32)
    upper = (i[:, None] <= i[None, :]).astype(np.float32)
    upper_ones = np.concatenate([upper, np.ones((P, P), np.float32)], 1)
    between = np.zeros((P, NLEV + 1, P), np.float32)
    pair = np.zeros((P, NLEV, P), np.float32)
    pair[:, 0] = ident
    for n in range(NLEV - 1):
        b = 1 << n
        mid = (i // (2 * b)) * 2 * b + b
        late = i >= mid
        s = i[:, None]
        between[:, n] = np.where(late, (s >= mid) & (s <= i), (s > i) & (s < mid))
        same = (i[:, None] // (2 * b)) == (i[None, :] // (2 * b))
        pair[:, n + 1] = same & ~late[:, None] & late[None, :]
    between[:, NLEV - 1] = i[:, None] > i[None, :]
    between[:, NLEV] = upper
    between /= 16.0
    causal = np.zeros((P, 2 * P), np.float32)
    causal[:, P:] = np.where(i[None, :] <= i[:, None], 0.0, MASKED)
    pick = np.zeros((FH, FH, P), np.float32)
    for h in range(FH):
        pick[h, h] = 1.0
    return {"c_ident": ident, "c_upper": upper_ones, "c_between": between.reshape(P, -1),
            "c_pair": pair.reshape(P, -1), "c_causal": causal, "c_pick": pick.reshape(FH, -1)}


def build(nc, a, out):
    with ExitStack() as ctx:
        def sb(name, shape, dt=F32):
            return ctx.enter_context(nc.sbuf_tensor(name, shape, dt))

        def sem(name):
            return ctx.enter_context(nc.semaphore(name))

        banks = ctx.enter_context(nc.psum_tensor("banks", [P, 8, 512], F32))
        acc = [banks[:, i, :] for i in range(4)]
        inb = [banks[:, 4 + i, :] for i in range(2)]
        tpb = [banks[:, 6 + i, :] for i in range(2)]
        flat = banks[:, :, :].rearrange("p b n -> p (b n)")

        raw = [sb(f"raw{i}", [P, 2048]) for i in range(RING)]
        whi = [sb(f"whi{i}", [P, 2048], F32R) for i in range(RING)]
        wlo = [sb(f"wlo{i}", [P, 2048], F32R) for i in range(RING)]
        xhi = [sb(f"xhi{i}", [P, KT, 256], F32R) for i in range(2)]
        xlo = [sb(f"xlo{i}", [P, KT, 256], F32R) for i in range(2)]
        gained = [sb(f"gained{i}", [P, 4, P]) for i in range(2)]
        h = sb("h", [P, T, D])
        gthi = sb("gthi", [P, 2, 256], F32R)
        gtlo = sb("gtlo", [P, 2, 256], F32R)
        squares = sb("squares", [P, 8, T])
        meansq = sb("meansq", [P, 8, T])
        rstd = sb("rstd", [P, 8, T])
        rstd_half = sb("rstd_half", [P, 8, T])
        rstd_sq_half = sb("rstd_sq_half", [P, 8, T])
        power = sb("power", [P, 8])
        ident = sb("ident", [P, P])
        upper = sb("upper", [P, 2 * P])
        gains_raw = sb("gains_raw", [72, P])
        gains = sb("gains", [P, 72])
        work = sb("work", [P, WORK])
        ghead = sb("ghead", [P, DV])
        memkv_l = [sb(f"memkv{l}", [P, T, 512]) for l in range(2)]
        mstat = sb("mstat", [P, 4, 16])

        cursor = [0]

        def carve(n, parts=P):
            s = cursor[0]
            cursor[0] += n
            assert cursor[0] <= WORK, cursor[0]
            return work[0:parts, s:s + n]

        mem = work[:, 0:T * D].rearrange("p (t n) -> p t n", t=T)
        th, half, gated = (work[:, WORK - 512 * (i + 1):WORK - 512 * i].rearrange("p (t n) -> p t n", t=T)
                           for i in range(3))
        pair_f32 = work[:, T * D:T * D + NLEV * P]
        scratch = work[:, WORK - D:WORK]
        gfinal = work[:, 0:D]

        mkT = carve(512).rearrange("p (a n) -> p a n", a=2)
        mqT = carve(512).rearrange("p (a n) -> p a n", a=2)
        mprob_flat, mprobT_flat = carve(2048), carve(2048)
        mprob = mprob_flat.rearrange("p (t h n) -> p t h n", t=2, h=4)
        mprobT = mprobT_flat.rearrange("p (k h n) -> p k h n", k=2, h=4)
        after_memory = cursor[0]
        pa = carve(T * 1552).rearrange("p (t n) -> p t n", t=T)
        v_gla = pa[:, :, 0:768]
        r_gla = pa[:, :, 768:1536]
        glow = pa[:, :, 1536:1552]
        qk_flat = carve(T * 1024)
        qk = qk_flat.rearrange("p (t n) -> p t n", t=T)
        qT = carve(1024, DK)
        kT = carve(1024, DK)
        gates = carve(2304)
        gmin, gneg, loga = (gates[:, 768 * i:768 * i + 768].rearrange("p (t n) -> p t n", t=T) for i in range(3))
        scores = carve(1024)
        cross = carve(512).rearrange("p (h n) -> p h n", h=GH)
        glT = mprob_flat[0:RANK, 0:256]
        joined = [mprob_flat[0:DK, 1024 * i:1024 * i + 1024] for i in range(2)]
        decay = [mprobT_flat[0:DK, 1024 * i:1024 * i + 1024] for i in range(2)]
        osquares = mprobT_flat[:, 0:T * GH * DV]
        sgate = qk_flat[:, 0:1536].rearrange("p (t n) -> p t n", t=T)
        ohead = gates[:, 0:1536].rearrange("p (t n) -> p t n", t=T)
        cursor[0] = after_memory
        kv = carve(T * 1536).rearrange("p (t n) -> p t n", t=T)
        qb_flat = carve(T * 1024)
        qb = qb_flat.rearrange("p (t n) -> p t n", t=T)
        fkT_flat = carve(1536)
        fkT = fkT_flat.rearrange("p (h n) -> p h n", h=FH)
        fqT = carve(1536).rearrange("p (h n) -> p h n", h=FH)
        fprob0 = carve(768).rearrange("p (h n) -> p h n", h=FH)
        fprob1 = carve(1536).rearrange("p (h n) -> p h n", h=FH)
        fprobT0 = qb_flat[:, 0:1536].rearrange("p (h n) -> p h n", h=FH)
        fprobT1 = fkT_flat[:, 0:768].rearrange("p (h n) -> p h n", h=FH)

        between = sb("between", [P, (NLEV + 1) * P])
        pair = sb("pair", [P, NLEV * P], U8)
        causal = sb("causal", [P, 2 * P])
        pick_rows = sb("pick_rows", [33, FH * P])
        pick, ones_row = pick_rows[0:FH, :], pick_rows[32:33, 0:P]
        gate_rows = sb("gate_rows", [33, GH * DK])
        wgate, bgate = gate_rows[0:RANK, :], gate_rows[32:33, :]
        bf = sb("bf", [P, FH])
        fg = sb("fg", [P, 4, T, FH])
        negD = sb("negD", [FH, 256])
        Dtok = sb("Dtok", [P, T, FH])
        fstat = sb("fstat", [P, 4, T * FH])
        ostat = sb("ostat", [P, 3, T * GH])

        raw_landed = [sem(f"raw_landed{i}") for i in range(RING)]
        hi_ready = sem("hi_ready")
        lo_ready = sem("lo_ready")
        halves_done = sem("halves_done")
        x_landed = [sem(f"x_landed{t}") for t in range(T)]
        mem_landed = sem("mem_landed")
        ident_landed = sem("ident_landed")
        gains_landed = sem("gains_landed")
        const_landed = sem("const_landed")
        final_landed = sem("final_landed")
        gainsT_ready = sem("gainsT_ready")
        gains_ready = sem("gains_ready")
        normT_ready = sem("normT_ready")
        gained_ready = sem("gained_ready")
        xhi_ready = sem("xhi_ready")
        xlo_ready = sem("xlo_ready")
        squares_ready = sem("squares_ready")
        meansq_ready = sem("meansq_ready")
        rstd_ready = sem("rstd_ready")
        half_ready = sem("half_ready")
        stats_ready = sem("stats_ready")
        power_set = sem("power_set")
        ones_set = sem("ones_set")
        th_ready = sem("th_ready")
        y_ready = sem("y_ready")
        g_ready = sem("g_ready")
        gT_ready = sem("gT_ready")
        gthi_ready = sem("gthi_ready")
        gtlo_ready = sem("gtlo_ready")
        chunk_taken = sem("chunk_taken")
        h_updated = sem("h_updated")
        glT_ready, glT_taken = sem("glT_ready"), sem("glT_taken")
        gate_product = sem("gate_product")
        pair_ready = sem("pair_ready")
        gate_ready, gmin_ready, gneg_ready = sem("gate_ready"), sem("gmin_ready"), sem("gneg_ready")
        gexp_ready, gln_ready, loga_ready = sem("gexp_ready"), sem("gln_ready"), sem("loga_ready")
        qkT_ready, qkT_taken = sem("qkT_ready"), sem("qkT_taken")
        span_ready, decay_ready = sem("span_ready"), sem("decay_ready")
        joined_ready, score_ready, score_taken = sem("joined_ready"), sem("score_ready"), sem("score_taken")
        scores_zero = sem("scores_zero")
        o_ready, osq_ready, omean_ready, orstd_ready = (sem("o_ready"), sem("osq_ready"),
                                                        sem("omean_ready"), sem("orstd_ready"))
        rth_ready, rsilu_ready, sgate_ready, ohead_ready = (sem("rth_ready"), sem("rsilu_ready"),
                                                            sem("sgate_ready"), sem("ohead_ready"))
        oT_ready, oThi_ready, oTlo_ready = sem("oT_ready"), sem("oThi_ready"), sem("oTlo_ready")
        mT_ready, mT_taken = sem("mT_ready"), sem("mT_taken")
        ms_ready, mmax_ready, mneg_ready = sem("ms_ready"), sem("mmax_ready"), sem("mneg_ready")
        mexp_ready, mrecip_ready, mprob_ready = sem("mexp_ready"), sem("mrecip_ready"), sem("mprob_ready")
        mpT_ready, mpT_taken = sem("mpT_ready"), sem("mpT_taken")
        mo_ready, mohi_ready, molo_ready = sem("mo_ready"), sem("mohi_ready"), sem("molo_ready")
        fg_logit, fg_min, fg_neg, fg_exp, fg_ln, fg_log = (sem("fg_logit"), sem("fg_min"), sem("fg_neg"),
                                                          sem("fg_exp"), sem("fg_ln"), sem("fg_log"))
        cum_ready, cum_taken = sem("cum_ready"), sem("cum_taken")
        fT_ready, fT_taken = sem("fT_ready"), sem("fT_taken")
        fs_ready, flogit_ready, fmax_ready, fneg_ready = (sem("fs_ready"), sem("flogit_ready"),
                                                          sem("fmax_ready"), sem("fneg_ready"))
        fexp_ready, frecip_ready, fprob_ready = sem("fexp_ready"), sem("frecip_ready"), sem("fprob_ready")
        fpT_ready, fpT_taken = sem("fpT_ready"), sem("fpT_taken")
        fo_ready, fohi_ready, folo_ready = sem("fo_ready"), sem("fohi_ready"), sem("folo_ready")
        out_ready, out_stored = sem("out_ready"), sem("out_stored")

        def rows(w):
            return w.rearrange("(k p) n -> p k n", p=P)

        units = {}
        for l in range(2):
            for u in range(2):
                units[S_MK[l] + u] = (rows(a["w_mem_kv"][l])[:, 4 * u:4 * u + 4, :], 4, 512)
            for u, k in enumerate(OUT_ORDER):
                units[S_WO[l] + u] = (rows(a["w_out"][l])[:, k:k + 2, :], 2, D)
        for c, (at, wide) in enumerate(A_CHUNKS):
            for u in range(2):
                units[S_PA[c] + u] = (rows(a["w_in_a"][0])[:, 4 * u:4 * u + 4, at:at + wide], 4, wide)
        for c in range(3):
            for u in range(2):
                units[S_KV[c] + u] = (rows(a["w_kv_shared"])[:, 4 * u:4 * u + 4, 512 * c:512 * c + 512], 4, 512)
        units[S_FG] = (rows(a["w_fgate"]), KT, FH)
        for c in range(2):
            for u in range(2):
                units[S_PB + 2 * c + u] = (rows(a["w_in_b"][0])[:, 4 * u:4 * u + 4, 512 * c:512 * c + 512], 4, 512)

        def size(n):
            return units[n][1] * units[n][2] if n in units else 2048

        def slot_view(ring, n):
            _, k, wide = units[n]
            return ring[n % RING][:, 0:k * wide].rearrange("p (k n) -> p k n", k=k)

        ffn_in = [a["w_ffn_in"][f // 2, f % 2].rearrange("(k p) (s n) -> p k s n", p=P, s=2) for f in range(4)]
        ffn_out = [a["w_ffn_out"][f // 2, f % 2].rearrange("(j k p) n -> j p k n", p=P, k=2) for f in range(4)]

        block = ctx.enter_context(nc.Block())

        @block.sync
        def _(sp):
            def load(dst, src, signal):
                sp.dma_start(dst, src).then_inc(signal, 16)

            def claim(base, j=0):
                if not isinstance(j, int) or base >= RING:
                    sp.wait_ge(lo_ready, base + 3 * j - RING + 1)

            def load_in(f, u, base, step, j=0):
                claim(base, j)
                dst = raw[base % RING][:, :].rearrange("p (k s n) -> p k s n", k=4, s=2)
                col = step * 256
                for s in range(2):
                    sp.dma_start(dst[:, :, s, :], ffn_in[f][:, 4 * u:4 * u + 4, s, bass.ds(col, 256)]).then_inc(
                        raw_landed[base % RING], 16)

            def load_out(f, base, step, j=0):
                claim(base, j)
                dst = raw[base % RING][:, :].rearrange("p (k n) -> p k n", k=2)
                src = ffn_out[f][bass.ds(step, 1)].rearrange("a p k n -> p (a k) n")
                load(dst, src, raw_landed[base % RING])

            def load_unit(n):
                claim(n)
                load(slot_view(raw, n), units[n][0], raw_landed[n % RING])

            def load_ffn(f):
                B = S_FFN[f]
                load_in(f, 0, B, 0)
                load_in(f, 1, B + 1, 0)
                load_in(f, 0, B + 2, 1)
                load_in(f, 1, B + 3, 1)
                load_out(f, B + 4, 0)
                with sp.Fori(2, STEPS) as j:
                    load_in(f, 0, B - 1, j, j)
                    load_in(f, 1, B, j, j)
                    load_out(f, B + 1, j - 1, j)
                load_out(f, B + FFN_UNITS - 1, STEPS - 1)

            mixer_consts = [(upper[:], a["c_upper"]), (between[:], a["c_between"]), (pair_f32, a["c_pair"]),
                               (causal[:], a["c_causal"]), (pick, a["c_pick"]), (wgate, a["w_gate_up"][0]),
                               (bgate, a["b_gate"]),
                               (ghead[:], a["norm_gla_head"][0:1, :].to_broadcast([P, DV])),
                               (bf[:], a["b_fgate"].rearrange("(a n) -> a n", a=1).to_broadcast([P, FH]))]
            B = S_FFN[0]
            xr = a["x"][0].rearrange("(t p) d -> p t d", p=P)
            load(h[:, 0, :], xr[:, 0, :], x_landed[0])
            load(ident[:], a["c_ident"], ident_landed)
            load_in(0, 0, B, 0)
            load(h[:, 1, :], xr[:, 1, :], x_landed[1])
            load_in(0, 1, B + 1, 0)
            load(mem[:, :, :], a["mem"][0].rearrange("(t p) d -> p t d", p=P), mem_landed)
            load_in(0, 0, B + 2, 1)
            load_in(0, 1, B + 3, 1)
            load_out(0, B + 4, 0)
            with sp.Fori(2, STEPS) as j:
                load_in(0, 0, B - 1, j, j)
                load_in(0, 1, B, j, j)
                load_out(0, B + 1, j - 1, j)
            for dst, src in mixer_consts:
                load(dst, src, const_landed)
            load_out(0, B + FFN_UNITS - 1, STEPS - 1)
            for n in range(S_MK0, S_FFN1):
                load_unit(n)
            load_ffn(1)
            load_ffn(2)
            for n in range(S_KV[0], S_FFN3):
                load_unit(n)
            sp.wait_ge(folo_ready, 3)
            sp.wait_ge(molo_ready, 2)
            sp.dma_start(gfinal, a["norm_final"].rearrange("(a n) -> a n", a=1).to_broadcast([P, D])).then_inc(
                final_landed, 16)
            load_ffn(3)
            for t in range(T):
                for c in range(2):
                    cols = slice(512 * c, 512 * c + 512)
                    sp.wait_ge(out_ready, 2 * t + c + 1)
                    sp.dma_start(out[0].rearrange("(t p) d -> t p d", p=P)[t][:, cols],
                                 h[:, t, cols]).then_inc(out_stored, 16)
            sp.wait_ge(out_stored, 16 * 2 * T)

        def landed(n):
            total = 0
            for m in range(n % RING, n + 1, RING):
                total += 32 if is_input(m) else 16
            return total

        def is_input(n):
            for B in S_FFN:
                if B <= n < B + FFN_UNITS:
                    r = n - B
                    return r != FFN_UNITS - 1 and (r < 2 or r % 3 != 1)
            return False

        @block.tensor
        def _(pe):
            def split_matmul(dst, lh, ll, rh, rl, start, stop):
                nc.tensor.matmul(dst, lh, rh, start=start, stop=False)
                nc.tensor.matmul(dst, lh, rl, start=False, stop=False)
                return nc.tensor.matmul(dst, ll, rh, start=False, stop=stop)

            def norm_transposes(s, tiles=range(T)):
                src, _, _ = NORMS[s]
                rows_of = mem if src == "mem" else h
                for t in tiles:
                    if src == "x":
                        pe.wait_ge(x_landed[t], 16)
                    elif src == "mem":
                        pe.wait_ge(mem_landed, 16)
                    else:
                        pe.wait_ge(h_updated, 2 * H_UPDATES_BEFORE[s] + t - 1)
                    for g in range(2):
                        i = 4 * s + 2 * t + g
                        if i >= 4:
                            pe.wait_ge(gained_ready, i - 3)
                        for k in range(4):
                            last = nc.tensor.transpose(acc[2 * t + g][:, k * P:k * P + P],
                                                       rows_of[:, t, (4 * g + k) * P:(4 * g + k + 1) * P], ident[:])
                        last.then_inc(normT_ready, 1)

            def proj_unit(n, xset, k0, chunk_start, chunk_end, s, j=0, bank_free=None, hooks=None):
                if n in units and isinstance(j, int):
                    _, kn, wide = units[n]
                else:
                    kn, wide = 4, 512
                hi_v = whi[n % RING][:, 0:kn * wide].rearrange("p (k n) -> p k n", k=kn)
                lo_v = wlo[n % RING][:, 0:kn * wide].rearrange("p (k n) -> p k n", k=kn)
                pe.wait_ge(lo_ready, n + 3 * j + 1)
                for t in range(T):
                    if bank_free:
                        bank_free(t)
                    if s is not None:
                        pe.wait_ge(xlo_ready, 4 * s + 2 * t + (k0 + kn) // 4)
                    for k in range(kn):
                        if hooks and (t, k) in hooks:
                            hooks[t, k]()
                        c = k0 + k
                        last = split_matmul(inb[t][:, 0:wide], xhi[xset][:, c, t * P:t * P + P],
                                            xlo[xset][:, c, t * P:t * P + P], hi_v[:, k, :], lo_v[:, k, :],
                                            chunk_start and k == 0, chunk_end and k == kn - 1)
                    last.then_inc(halves_done, 1)

            def out_unit(n, lh, ll, first, final, j=0, hooks=None):
                hi_v = whi[n % RING][:, :].rearrange("p (k n) -> p k n", k=2)
                lo_v = wlo[n % RING][:, :].rearrange("p (k n) -> p k n", k=2)
                pe.wait_ge(lo_ready, n + 3 * j + 1)
                for t in range(T):
                    for k in range(2):
                        if hooks and (t, k) in hooks:
                            hooks[t, k]()
                        for c in range(2):
                            last = split_matmul(acc[2 * t + c], lh[:, k, t * P:t * P + P], ll[:, k, t * P:t * P + P],
                                                hi_v[:, k, 512 * c:512 * c + 512], lo_v[:, k, 512 * c:512 * c + 512],
                                                first and k == 0, final and k == 1)
                    last.then_inc(halves_done, 1)

            def gate_transposes(f, j):
                pe.wait_ge(g_ready, 2 * (STEPS * f) + 2 * j + 2)
                for c in range(2):
                    for t in range(T):
                        last = nc.tensor.transpose(tpb[0][:, c * 256 + t * P:c * 256 + t * P + P],
                                                   gated[:, t, c * P:c * P + P], ident[:])
                last.then_inc(gT_ready, 1)

            def ffn(f, s):
                B = S_FFN[f]

                def into(base, j=0):
                    proj_unit(base, X, 0, True, False, None, j)
                    proj_unit(base + 1, X, 4, False, True, None, j)

                def outof(base, step, j, first=False):
                    pe.wait_ge(gtlo_ready, STEPS * f + step + 1)
                    out_unit(base, gthi, gtlo, first, False, j)

                hooks = {(0, 2): lambda: norm_transposes(s, (1,))} if f > 0 else {}
                if f in (0, 2):
                    hooks[1, 2] = lambda: norm_transposes(1 if f == 0 else 6, (0,))
                proj_unit(B, X, 0, True, False, s, hooks=hooks)
                if f in (0, 2):
                    norm_transposes(1 if f == 0 else 6, (1,))
                proj_unit(B + 1, X, 4, False, True, s)
                proj_unit(B + 2, X, 0, True, False, None, bank_free=lambda t: pe.wait_ge(
                    g_ready, 2 * (STEPS * f) + t + 1))
                gate_transposes(f, 0)
                proj_unit(B + 3, X, 4, False, True, None)
                pe.wait_ge(gained_ready, 4 * (s + 1 + (f in (0, 2))))
                outof(B + 4, 0, 0, first=True)
                gate_transposes(f, 1)
                with pe.Fori(2, STEPS - 1) as j:
                    into(B - 1, j)
                    outof(B + 1, j - 1, j)
                    gate_transposes(f, j)
                into(B + FFN_UNITS - 4)
                pe.wait_ge(gtlo_ready, STEPS * f + STEPS - 1)
                out_unit(B + FFN_UNITS - 2, gthi, gtlo, False, False,
                         hooks={(1, 0): lambda: gate_transposes(f, STEPS - 1)})
                pe.wait_ge(gtlo_ready, STEPS * f + STEPS)
                out_unit(B + FFN_UNITS - 1, xhi[X][:, 0:2, :], xlo[X][:, 0:2, :], False, True,
                         hooks={(1, 1): lambda: norm_transposes(5, (0,))} if f == 1 else None)

            def chunk_free(c, t=1):
                pe.wait_ge(chunk_taken, 2 * c - 1 + t)

            def mem_operands(l):
                for i, (src, at) in enumerate([(memkv_l[l], 0), (qk if l == 0 else qb, 768)]):
                    for c in range(2):
                        for t in range(T):
                            last = nc.tensor.transpose(tpb[i][:, c * 256 + t * P:c * 256 + t * P + P],
                                                       src[:, t, at + c * P:at + c * P + P], ident[:])
                    last.then_inc(mT_ready, 1)

            def mem_scores(l, t):
                pe.wait_ge(mT_taken, 2 * l + 2)
                for m in range(MH):
                    p0 = MD * (m % 2)
                    at = t * 1024 + MEM_AT[m] * 256
                    last = nc.tensor.matmul(flat[:, at:at + 256],
                                            mqT[p0:p0 + MD, m // 2, t * P:t * P + P],
                                            mkT[p0:p0 + MD, m // 2, :], start=True, stop=True)
                last.then_inc(ms_ready, 1)

            def mem_weights(l):
                for i in range(4):
                    kt, c = i // 2, i % 2
                    if i == 0:
                        pe.wait_ge(mprob_ready, 2 * l + 2)
                    if i >= 2:
                        pe.wait_ge(mpT_taken, 4 * l + i - 1)
                    for m in range(2):
                        for t in range(T):
                            last = nc.tensor.transpose(tpb[i % 2][:, m * 256 + t * P:m * 256 + t * P + P],
                                                       mprob[:, t, 2 * c + m, kt * P:kt * P + P], ident[:])
                    last.then_inc(mpT_ready, 1)

            def mem_values(l):
                pe.wait_ge(mpT_taken, 4 * l + 4)
                for c in range(2):
                    for m in range(2):
                        for kt in range(2):
                            mh = 2 * c + m
                            last = nc.tensor.matmul(tpb[0][MD * m:MD * m + MD, c * 256:c * 256 + 256],
                                                    memkv_l[l][:, kt, 256 + MD * mh:256 + MD * mh + MD],
                                                    mprobT[:, kt, mh, :], start=(kt == 0), stop=(kt == 1))
                last.then_inc(mo_ready, 1)

            pe.wait_ge(ident_landed, 16)
            pe.wait_ge(gains_landed, 64)
            nc.tensor.transpose(tpb[0][:, 0:72], gains_raw[:, :], ident[0:72, 0:72]).then_inc(gainsT_ready, 1)
            norm_transposes(0)
            ffn(0, 0)

            proj_unit(S_MK0, Y, 0, True, False, 1)
            norm_transposes(2)
            proj_unit(S_MK0 + 1, Y, 4, False, True, 1)

            def spans(n):
                if n == 0:
                    pe.wait_ge(loga_ready, 2)
                    pe.wait_ge(gained_ready, 16)
                else:
                    pe.wait_ge(decay_ready, n)
                for hh in range(GH):
                    for t in range(T):
                        m = n + (t if n == NLEV - 1 else 0)
                        at = (hh * 2 + t) * P
                        last = nc.tensor.matmul(flat[0:DK, at:at + P], loga[:, t, hh * DK:hh * DK + DK],
                                                between[:, m * P:m * P + P], start=True, stop=True)
                last.then_inc(span_ready, 1)

            def level_scores(n):
                if n >= 1:
                    pe.wait_ge(joined_ready, n)
                    pe.wait_ge(score_taken, n)
                w = joined[(n - 1) % 2]
                if n == NLEV:
                    for hh in range(GH):
                        at = hh * 256
                        last = nc.tensor.matmul(flat[:, 1024 + hh * P:1024 + hh * P + P], w[:, at:at + P],
                                                w[:, at + P:at + 256], start=True, stop=True)
                else:
                    for i in range(GH * T):
                        lhs = kT if n == 0 else w
                        rhs = qT if n == 0 else w
                        last = nc.tensor.matmul(flat[:, 1024 + i * P:1024 + i * P + P], lhs[:, i * P:i * P + P],
                                                rhs[:, i * P:i * P + P], start=True, stop=True)
                last.then_inc(score_ready, 1)

            def head_transposes(w):
                for t in range(T):
                    pe.wait_ge(gneg_ready, 2) if w == 0 else pe.wait_ge(qkT_taken, t + 1)
                    for hh in range(GH):
                        at = w * 384 + hh * DK
                        last = nc.tensor.transpose(tpb[t][0:DK, hh * P:hh * P + P], qk[:, t, at:at + DK], ident[:])
                    last.then_inc(qkT_ready, 1)

            proj_unit(S_PA[0], X, 0, True, False, 2, bank_free=lambda t: chunk_free(1))
            norm_transposes(3)
            proj_unit(S_PA[0] + 1, X, 4, False, True, 2)
            proj_unit(S_PA[1], X, 0, True, False, 2, bank_free=lambda t: chunk_free(2, t))
            for t in range(T):
                last = nc.tensor.transpose(tpb[0][0:RANK, t * P:t * P + P], glow[:, t, :], ident[:])
            last.then_inc(glT_ready, 1)
            proj_unit(S_PA[1] + 1, X, 4, False, True, 2)
            pe.wait_ge(glT_taken, 1)
            mem_operands(0)
            proj_unit(S_PA[2], X, 0, True, False, 2, bank_free=lambda t: chunk_free(3, t))
            pe.wait_ge(const_landed, 16 * 9)
            pe.wait_ge(ones_set, 1)
            pe.wait_ge(mT_taken, 2)
            for t in range(T):
                nc.tensor.matmul(tpb[t][:, 0:GH * DK], glT[:, t * P:t * P + P], wgate,
                                 start=True, stop=False).then_inc(gate_product, 1)
                pe.wait_ge(gate_product, t + 1)
                nc.tensor.matmul(tpb[t][:, 0:GH * DK], ones_row, bgate,
                                 start=False, stop=True).then_inc(gate_ready, 1)
            proj_unit(S_PA[2] + 1, X, 4, False, True, 2)
            proj_unit(S_MK1, Y, 0, True, False, 3, bank_free=lambda t: chunk_free(4, t))
            head_transposes(0)
            head_transposes(1)
            proj_unit(S_MK1 + 1, Y, 4, False, True, 3)
            spans(0)
            for c in range(3, 6):
                proj_unit(S_PA[c], X, 0, True, False, 2, bank_free=lambda t: chunk_free(2 + c, t))
                spans(2 * c - 5)
                if c == 3:
                    pe.wait_ge(qkT_taken, 4)
                level_scores(2 * c - 6)
                proj_unit(S_PA[c] + 1, X, 4, False, True, 2)
                spans(2 * c - 4)
                level_scores(2 * c - 5)
            spans(NLEV - 1)
            level_scores(NLEV - 2)
            level_scores(NLEV - 1)
            pe.wait_ge(decay_ready, NLEV)
            mem_scores(0, 0)
            level_scores(NLEV)
            pe.wait_ge(score_taken, NLEV + 1)
            chunk_free(8)
            mem_scores(0, 1)
            for t in range(T):
                if t == 1:
                    pe.wait_ge(mexp_ready, 4)
                for hh in range(GH):
                    dst = flat[:, gla_at(t, hh):gla_at(t, hh) + DV]
                    last = nc.tensor.matmul(dst, scores[:, (hh * 2 + t) * P:(hh * 2 + t + 1) * P],
                                            v_gla[:, t, hh * DV:hh * DV + DV], start=True, stop=(t == 0))
                    if t == 1:
                        last = nc.tensor.matmul(dst, cross[:, hh, :], v_gla[:, 0, hh * DV:hh * DV + DV],
                                                start=False, stop=True)
                last.then_inc(o_ready, 1)
            mem_weights(0)
            pe.wait_ge(mpT_taken, 4)
            for i in range(4):
                t, g = i // 2, i % 2
                pe.wait_ge(ohead_ready, t + 1)
                if i >= 2:
                    pe.wait_ge(oTlo_ready, i - 1)
                for k in range(4 if g == 0 else 2):
                    c = 4 * g + k
                    last = nc.tensor.transpose(tpb[g][:, k * P:k * P + P], ohead[:, t, c * P:c * P + P], ident[:])
                last.then_inc(oT_ready, 1)
            pe.wait_ge(oTlo_ready, 4)
            for u, k in enumerate(OUT_ORDER):
                if u == 1:
                    mem_values(0)
                if k == 6:
                    pe.wait_ge(molo_ready, 1)
                out_unit(S_WO0 + u, xhi[Y][:, k:k + 2, :], xlo[Y][:, k:k + 2, :], u == 0, u == 3,
                         hooks={(1, 1): lambda: norm_transposes(4, (0,))} if u == 3 else None)
            ffn(1, 4)

            ffn(2, 5)

            def fox_transposes(groups):
                for i in groups:
                    src = kv if i < 3 else qb
                    pe.wait_ge(fT_taken, i - 1) if i >= 2 else pe.wait_ge(cum_taken, 2)
                    for m in range(2):
                        for t in range(T):
                            hh = 2 * (i % 3) + m
                            last = nc.tensor.transpose(tpb[i % 2][:, m * 256 + t * P:m * 256 + t * P + P],
                                                       src[:, t, hh * FD:hh * FD + FD], ident[:])
                    last.then_inc(fT_ready, 1)

            proj_unit(S_KV[0], Y, 0, True, False, 6)
            norm_transposes(7)
            proj_unit(S_KV[0] + 1, Y, 4, False, True, 6)
            proj_unit(S_KV[1], Y, 0, True, False, 6, bank_free=lambda t: chunk_free(9, t))
            proj_unit(S_KV[1] + 1, Y, 4, False, True, 6)
            proj_unit(S_FG, Y, 0, True, True, 6, bank_free=lambda t: chunk_free(10, t))
            proj_unit(S_PB, X, 0, True, False, 7, bank_free=lambda t: chunk_free(11, t))
            proj_unit(S_PB + 1, X, 4, False, True, 7)
            pe.wait_ge(fg_log, 1)
            logf = fg[:, 3]
            nc.tensor.matmul(tpb[0][0:FH, 0:256], logf[:, 0, :], upper[:], start=True, stop=False)
            nc.tensor.matmul(tpb[0][0:FH, P:256], logf[:, 1, :], upper[:, 0:P],
                             start=False, stop=True).then_inc(cum_ready, 1)
            nc.tensor.matmul(tpb[1][:, 0:FH], upper[:, 0:P], logf[:, 0, :], start=True, stop=True)
            nc.tensor.matmul(tpb[1][:, 8:8 + FH], upper[:, P:256], logf[:, 0, :], start=True, stop=False)
            nc.tensor.matmul(tpb[1][:, 8:8 + FH], upper[:, 0:P], logf[:, 1, :],
                             start=False, stop=True).then_inc(cum_ready, 1)
            proj_unit(S_PB + 2, X, 0, True, False, 7, bank_free=lambda t: chunk_free(12, t))
            fox_transposes(range(0, 2))
            proj_unit(S_PB + 3, X, 4, False, True, 7)
            fox_transposes(range(2, 4))
            proj_unit(S_KV[2], Y, 0, True, False, 6, bank_free=lambda t: chunk_free(13, t))
            fox_transposes(range(4, 6))
            pe.wait_ge(fT_taken, 6)
            def fox_scores(t):
                wide = P * (t + 1)
                for hh in range(FH):
                    at = fox_at(t, hh)
                    nc.tensor.matmul(flat[:, at:at + wide], fqT[:, hh, t * P:t * P + P], fkT[:, hh, 0:wide],
                                     start=True, stop=False)
                    last = nc.tensor.matmul(flat[:, at:at + wide], pick[:, hh * P:hh * P + P], negD[:, 0:wide],
                                            start=False, stop=True)
                last.then_inc(fs_ready, 1)

            fox_scores(1)
            mem_operands(1)
            proj_unit(S_KV[2] + 1, Y, 4, False, True, 6)
            pe.wait_ge(mT_taken, 4)
            fox_scores(0)
            pe.wait_ge(flogit_ready, 1)
            mem_scores(1, 0)
            pe.wait_ge(flogit_ready, 2)
            mem_scores(1, 1)
            pe.wait_ge(fprob_ready, 2)
            for i in range(5):
                if i >= 2:
                    pe.wait_ge(fpT_taken, i - 1)
                if i < 3:
                    for m in range(2):
                        for t in range(T):
                            p = (fprob0 if t == 0 else fprob1)[:, 2 * i + m, 0:P]
                            last = nc.tensor.transpose(tpb[i % 2][:, m * 256 + t * P:m * 256 + t * P + P], p, ident[:])
                else:
                    for m in range(4 if i == 3 else 2):
                        hh = 4 * (i - 3) + m
                        last = nc.tensor.transpose(tpb[i % 2][:, m * P:m * P + P], fprob1[:, hh, P:2 * P], ident[:])
                last.then_inc(fpT_ready, 1)
            pe.wait_ge(fpT_taken, 5)
            chunk_free(14)
            pe.wait_ge(mexp_ready, 16)
            for c in range(3):
                for m in range(2):
                    hh = 2 * c + m
                    v0 = 768 + hh * FD
                    nc.tensor.matmul(acc[c][:, m * 256:m * 256 + 256], kv[:, 0, v0:v0 + FD], fprobT0[:, hh, :],
                                     start=True, stop=False)
                    last = nc.tensor.matmul(acc[c][:, m * 256 + P:m * 256 + 256], kv[:, 1, v0:v0 + FD],
                                            fprobT1[:, hh, :], start=False, stop=True)
                last.then_inc(fo_ready, 1)
            mem_weights(1)
            pe.wait_ge(folo_ready, 3)
            for u, k in enumerate(OUT_ORDER):
                if u == 1:
                    mem_values(1)
                if k == 6:
                    pe.wait_ge(molo_ready, 2)
                out_unit(S_WO1 + u, xhi[Y][:, k:k + 2, :], xlo[Y][:, k:k + 2, :], u == 0, u == 3,
                         hooks={(1, 1): lambda: norm_transposes(8, (0,))} if u == 3 else None)
            ffn(3, 8)

        @block.scalar
        def _(act):
            following = [0]

            def split_hi(base, j=0, due=None):
                act.wait_ge(raw_landed[base % RING], due)
                if not isinstance(j, int) or base >= RING:
                    act.wait_ge(halves_done, 2 * (base + 3 * j - RING + 1))
                n = size(base) if isinstance(j, int) else 2048
                nc.scalar.copy(whi[base % RING][:, 0:n], raw[base % RING][:, 0:n]).then_inc(hi_ready, 1)

            def split(n):
                assert n == following[0]
                following[0] += 1
                if n < S_END:
                    split_hi(n, 0, landed(n))

            def split_next():
                if following[0] < S_END:
                    split(following[0])

            def norm_hi(s, tiles=range(T)):
                xset = NORMS[s][2]
                for i in [4 * s + 2 * t + g for t in tiles for g in range(2)]:
                    t, g = (i % 4) // 2, i % 2
                    act.wait_ge(gained_ready, i + 1)
                    nc.scalar.copy(xhi[xset][:, 4 * g:4 * g + 4, t * P:t * P + P],
                                   gained[i % 2][:, :, :]).then_inc(xhi_ready, 1)

            def square_sums(st, rows_of, discard):
                for t in range(T):
                    if 2 * st + t:
                        act.wait_ge(squares_ready, 2 * st + t)
                    nc.scalar.activation(discard, rows_of[:, t, :], ACT.Square,
                                         accum_out=squares[:, st, t:t + 1]).then_inc(squares_ready, 1)

            def gate_hi(f, j):
                last_step = isinstance(j, int) and j == STEPS - 1
                dst = xhi[X][:, 0:2, :] if last_step else gthi[:, :, :]
                act.wait_ge(gT_ready, STEPS * f + j + 1)
                nc.scalar.copy(dst.rearrange("p c n -> p (c n)"), tpb[0]).then_inc(gthi_ready, 1)

            def tanh_in(f, st, base, j, tiles=range(T)):
                for t in tiles:
                    act.wait_ge(halves_done, 2 * base + 6 * j + t + 1)
                    nc.scalar.activation(th[:, t, :], inb[t][:, 0:256], ACT.Tanh,
                                         scale=rstd_half[:, st, t:t + 1]).then_inc(th_ready, 1)

            def ffn(f, st):
                B = S_FFN[f]
                assert following[0] == B + 2
                split_next()
                act.wait_ge(stats_ready, st + 1)
                act.wait_ge(squares_ready, 2 * st + 2)
                for t in range(T):
                    if f in (0, 2):
                        norm_hi(1 if f == 0 else 6, (t,))
                    tanh_in(f, st, B + 1, 0, (t,))
                split_next()
                gate_hi(f, 0)
                split_next()
                split_next()
                tanh_in(f, st, B + 3, 0)
                split_next()
                if f == 0:
                    square_sums(ST_MEM, mem, work[:, 4096:4096 + D])
                assert following[0] == B + 7
                with act.Fori(2, STEPS - 1) as j:
                    gate_hi(f, j - 1)
                    per = 32
                    split_hi(B + 1, j, landed(B + 1 + 6) + 16 * (j - 2))
                    split_hi(B + 2, j, landed(B + 2 + 6) + per * (j - 2))
                    tanh_in(f, st, B, j)
                    split_hi(B + 3, j, landed(B + 3 + 6) + per * (j - 2))
                following[0] += 3 * (STEPS - 3)
                gate_hi(f, STEPS - 2)
                split_next()
                split_next()
                tanh_in(f, st, B + 3 * (STEPS - 1), 0)
                gate_hi(f, STEPS - 1)
                split_next()
                split_next()
                assert following[0] == B + FFN_UNITS + 2 or following[0] == S_END

            def take_chunk(n, pieces, st):
                act.wait_ge(stats_ready, st + 1)
                for t in range(T):
                    act.wait_ge(halves_done, 2 * n + t + 1)
                    for i, (dst, lo, hi) in enumerate(pieces):
                        last = nc.scalar.activation(dst[:, t, :], inb[t][:, lo:hi], ACT.Copy,
                                                    scale=rstd[:, st, t:t + 1])
                    last.then_inc(chunk_taken, 1)

            def mem_take(l):
                act.wait_ge(mT_ready, 2 * l + 1)
                nc.scalar.copy(mkT.rearrange("p a n -> p (a n)"), tpb[0]).then_inc(mT_taken, 1)
                act.wait_ge(mT_ready, 2 * l + 2)
                nc.scalar.mul(mqT.rearrange("p a n -> p (a n)"), tpb[1], MD ** -0.5).then_inc(mT_taken, 1)

            def mem_exp(l, t):
                act.wait_ge(mneg_ready, 2 * l + t + 1)
                for m in range(MH):
                    at = t * 1024 + MEM_AT[m] * 256
                    i = 4 * t + MEM_AT[m]
                    nc.scalar.activation(mprob[:, t, m, :], flat[:, at:at + 256], ACT.Exp,
                                         bias=mstat[:, 1, i:i + 1],
                                         accum_out=mstat[:, 2, i:i + 1]).then_inc(mexp_ready, 1)

            def mem_probT(l):
                for i in range(4):
                    act.wait_ge(mpT_ready, 4 * l + i + 1)
                    kt, c = i // 2, i % 2
                    nc.scalar.copy(mprobT[:, kt, 2 * c:2 * c + 2, :].rearrange("p h n -> p (h n)"),
                                   tpb[i % 2]).then_inc(mpT_taken, 1)

            def mem_out_hi(l):
                act.wait_ge(mo_ready, l + 1)
                nc.scalar.copy(xhi[Y][:, 6:8, :].rearrange("p c n -> p (c n)"), tpb[0]).then_inc(mohi_ready, 1)

            row = 0
            for name in ("norm_ffn", "norm_mix", "norm_mem", "norm_shared"):
                src = a[name]
                if len(src.shape) == 3:
                    src = src.rearrange("a b c -> (a b) c")
                if len(src.shape) == 2:
                    src = src.rearrange("a c -> (a c)")
                src = src.rearrange("(a c) -> a c", c=P)
                act.dma_start(gains_raw[row:row + src.shape[0], :], src).then_inc(gains_landed, 16)
                row += src.shape[0]
            split_next()
            norm_hi(0, (0,))
            split_next()
            norm_hi(0, (1,))
            square_sums(ST_X, h, scratch)
            ffn(0, ST_X)

            split_next()
            norm_hi(2)
            split_next()
            take_chunk(S_MK0 + 1, [(memkv_l[0], 0, 512)], ST_MEM)
            split_next()
            act.wait_ge(h_updated, 2)
            square_sums(ST_H, h, scratch)
            split_next()

            take_chunk(S_PA[0] + 1, [(glow, 0, 16), (qk[:, :, 768:1024], 16, 272)], ST_H)
            norm_hi(3)
            split_next()
            split_next()
            take_chunk(S_PA[1] + 1, [(qk[:, :, 0:512], 0, 512)], ST_H)
            split_next()
            mem_take(0)
            split_next()
            for t in range(T):
                act.wait_ge(gneg_ready, t + 1)
                nc.scalar.activation(gneg[:, t, :], gneg[:, t, :], ACT.Exp).then_inc(gexp_ready, 1)
            for t in range(T):
                act.wait_ge(gexp_ready, t + 1)
                nc.scalar.activation(gneg[:, t, :], gneg[:, t, :], ACT.Ln, bias=1.0).then_inc(gln_ready, 1)
            take_chunk(S_PA[2] + 1, [(qk[:, :, 512:768], 0, 256), (v_gla[:, :, 0:256], 256, 512)], ST_H)
            split_next()

            def head_take(i):
                w, t = i // 2, i % 2
                act.wait_ge(qkT_ready, i + 1)
                dst = (qT if w == 0 else kT).rearrange("p (h t n) -> p h t n", h=GH, t=T)[:, :, t, :]
                src = tpb[t][0:DK, :].rearrange("p (h n) -> p h n", h=GH)
                nc.scalar.mul(dst, src, DK ** -0.5 if w == 0 else 1.0).then_inc(qkT_taken, 1)

            def decays(n):
                act.wait_ge(span_ready, n + 1)
                if n >= 2:
                    act.wait_ge(joined_ready, n - 1)
                nc.scalar.activation(decay[n % 2], flat[0:DK, 0:1024], ACT.Exp).then_inc(decay_ready, 1)

            for i in range(4):
                head_take(i)
            split_next()
            take_chunk(S_MK1 + 1, [(memkv_l[1], 0, 512)], ST_MEM)
            decays(0)
            split_next()
            decays(1)
            split_next()
            takes = [(v_gla[:, :, 256:768], 0, 512), (r_gla[:, :, 0:512], 0, 512), (r_gla[:, :, 512:768], 0, 256)]
            for c in range(3, 6):
                take_chunk(S_PA[c] + 1, [takes[c - 3]], ST_H)
                decays(2 * c - 4)
                split_next()
                if c < 5:
                    decays(2 * c - 3)
                    split_next()
            decays(NLEV - 1)
            mem_exp(0, 0)
            act.wait_ge(chunk_taken, 16)
            nc.scalar.activation(sgate[:, :, :], r_gla, ACT.Tanh, scale=0.5).then_inc(rth_ready, 1)
            for t in range(T):
                if t == 1:
                    mem_exp(0, 1)
                act.wait_ge(o_ready, t + 1)
                act.wait_ge(decay_ready, NLEV)
                for hh in range(GH):
                    i = GH * t + hh
                    nc.scalar.activation(osquares[:, i * DV:i * DV + DV], flat[:, gla_at(t, hh):gla_at(t, hh) + DV], ACT.Square,
                                         accum_out=ostat[:, 0, i:i + 1]).then_inc(osq_ready, 1)
            act.wait_ge(osq_ready, T * GH)
            mem_probT(0)
            for i in range(4):
                t, g = i // 2, i % 2
                k = 4 if g == 0 else 2
                act.wait_ge(oT_ready, i + 1)
                nc.scalar.copy(xhi[Y][:, 4 * g:4 * g + k, t * P:t * P + P],
                               tpb[g][:, 0:k * P].rearrange("p (k n) -> p k n", k=k)).then_inc(oThi_ready, 1)
            mem_out_hi(0)
            split_next()
            split_next()
            split_next()
            norm_hi(4)
            act.wait_ge(h_updated, 4)
            square_sums(ST_H + 1, h, scratch)
            ffn(1, ST_H + 1)

            norm_hi(5)
            act.wait_ge(h_updated, 6)
            square_sums(ST_H + 2, h, scratch)
            ffn(2, ST_H + 2)

            split_next()
            norm_hi(7)
            split_next()
            take_chunk(S_KV[0] + 1, [(kv[:, :, 0:512], 0, 512)], ST_H + 2)
            split_next()
            square_sums(ST_H + 3, h, scratch)
            split_next()
            take_chunk(S_KV[1] + 1, [(kv[:, :, 512:1024], 0, 512)], ST_H + 2)
            split_next()
            act.wait_ge(fg_neg, 1)
            nc.scalar.activation(fg[:, 2], fg[:, 1], ACT.Exp).then_inc(fg_exp, 1)
            act.wait_ge(fg_exp, 1)
            nc.scalar.activation(fg[:, 1], fg[:, 2], ACT.Ln, bias=1.0).then_inc(fg_ln, 1)
            split_next()
            split_next()
            take_chunk(S_PB + 1, [(qb[:, :, 0:512], 0, 512)], ST_H + 3)
            split_next()

            def fox_take(groups):
                for i in groups:
                    act.wait_ge(fT_ready, i + 1)
                    dst = (fkT if i < 3 else fqT)[:, 2 * (i % 3):2 * (i % 3) + 2, :].rearrange("p h n -> p (h n)")
                    nc.scalar.mul(dst, tpb[i % 2], 1.0 if i < 3 else FD ** -0.5).then_inc(fT_taken, 1)

            split_next()
            fox_take(range(0, 2))
            take_chunk(S_PB + 3, [(qb[:, :, 512:1024], 0, 512)], ST_H + 3)
            split_next()
            fox_take(range(2, 4))
            split_next()
            fox_take(range(4, 6))
            mem_take(1)
            take_chunk(S_KV[2] + 1, [(kv[:, :, 1024:1536], 0, 512)], ST_H + 2)
            for t in (1, 0):
                act.wait_ge(fneg_ready, 2 - t)
                p = fprob1 if t else fprob0
                for hh in range(FH):
                    i = FH * t + hh
                    nc.scalar.activation(p[:, hh, :], p[:, hh, :], ACT.Exp, bias=fstat[:, 1, i:i + 1],
                                         accum_out=fstat[:, 2, i:i + 1]).then_inc(fexp_ready, 1)
            mem_exp(1, 0)
            mem_exp(1, 1)
            split_next()
            for i in range(5):
                act.wait_ge(fpT_ready, i + 1)
                if i < 3:
                    dst, src = fprobT0[:, 2 * i:2 * i + 2, :], tpb[i % 2]
                elif i == 3:
                    dst, src = fprobT1[:, 0:4, :], tpb[i % 2]
                else:
                    dst, src = fprobT1[:, 4:6, :], tpb[i % 2][:, 0:256]
                nc.scalar.copy(dst.rearrange("p h n -> p (h n)"), src).then_inc(fpT_taken, 1)
            for c in range(3):
                act.wait_ge(fo_ready, c + 1)
                nc.scalar.copy(xhi[Y][:, 2 * c:2 * c + 2, :].rearrange("p c n -> p (c n)"),
                               acc[c]).then_inc(fohi_ready, 1)
            mem_probT(1)
            mem_out_hi(1)
            split_next()
            split_next()
            split_next()
            norm_hi(8)
            act.wait_ge(h_updated, 10)
            square_sums(ST_H + 4, h, scratch)
            ffn(3, ST_H + 4)
            for t in range(T):
                act.wait_ge(h_updated, 10 + t + 1)
                act.wait_ge(squares_ready, 2 * (ST_H + 5) + t)
                nc.scalar.activation(work[:, D:2 * D], h[:, t, :], ACT.Square,
                                     accum_out=squares[:, ST_H + 5, t:t + 1]).then_inc(squares_ready, 1)

        @block.gpsimd
        def _(pool):
            nc.gpsimd.memset(power[:], -0.5).then_inc(power_set, 1)
            pool.wait_ge(power_set, 1)
            nc.gpsimd.memset(ones_row, 1.0).then_inc(ones_set, 1)
            pool.wait_ge(ones_set, 1)

            def row_stats(st):
                pool.wait_ge(squares_ready, 2 * st + 2)
                nc.gpsimd.tensor_scalar(meansq[:, st, :], squares[:, st, :], 1.0 / D, EPS, ALU.mult,
                                        ALU.add).then_inc(meansq_ready, 1)
                pool.wait_ge(meansq_ready, st + 1)
                nc.gpsimd.tensor_tensor(rstd[:, st, :], meansq[:, st, :], power[:, 0:T],
                                        ALU.pow).then_inc(rstd_ready, 1)
                pool.wait_ge(rstd_ready, st + 1)
                nc.gpsimd.tensor_scalar(rstd_half[:, st, :], rstd[:, st, :], 0.5, 0.0, ALU.mult,
                                        ALU.add).then_inc(half_ready, 1)
                pool.wait_ge(half_ready, st + 1)
                nc.gpsimd.tensor_tensor(rstd_sq_half[:, st, :], rstd[:, st, :], rstd_half[:, st, :],
                                        ALU.mult).then_inc(stats_ready, 1)

            row_stats(ST_X)
            row_stats(ST_MEM)
            pool.wait_ge(const_landed, 16 * 9)
            nc.gpsimd.tensor_copy(pair[:], pair_f32).then_inc(pair_ready, 1)
            row_stats(ST_H)
            pool.wait_ge(normT_ready, 16)
            pool.wait_ge(h_updated, 2)
            nc.gpsimd.memset(scores, 0.0).then_inc(scores_zero, 1)
            for t in range(T):
                cols = slice(GH * t, GH * t + GH)
                pool.wait_ge(osq_ready, GH * (t + 1))
                nc.gpsimd.tensor_scalar(ostat[:, 1, cols], ostat[:, 0, cols], 1.0 / DV, EPS, ALU.mult,
                                        ALU.add).then_inc(omean_ready, 1)
                pool.wait_ge(omean_ready, t + 1)
                nc.gpsimd.tensor_tensor(ostat[:, 2, cols], ostat[:, 1, cols], power[:, 0:GH],
                                        ALU.pow).then_inc(orstd_ready, 1)
            for st in range(ST_H + 1, ST_H + 5):
                row_stats(st)
            st = ST_H + 5
            for t in range(T):
                pool.wait_ge(squares_ready, 2 * st + t + 1)
                nc.gpsimd.tensor_scalar(meansq[:, st, t:t + 1], squares[:, st, t:t + 1], 1.0 / D, EPS, ALU.mult,
                                        ALU.add).then_inc(meansq_ready, 1)
                pool.wait_ge(meansq_ready, st + t + 1)
                nc.gpsimd.tensor_tensor(rstd[:, st, t:t + 1], meansq[:, st, t:t + 1], power[:, 0:1],
                                        ALU.pow).then_inc(rstd_ready, 1)

        @block.vector
        def _(dve):
            following = [0]

            def split_lo(base, j=0):
                dve.wait_ge(hi_ready, base + 3 * j + 1)
                n = size(base) if isinstance(j, int) else 2048
                r = base % RING
                nc.vector.tensor_tensor(wlo[r][:, 0:n], raw[r][:, 0:n], whi[r][:, 0:n].bitcast(F32),
                                        ALU.subtract).then_inc(lo_ready, 1)

            def split_next():
                if following[0] < S_END:
                    split_lo(following[0])
                    following[0] += 1

            def norm_gain(i):
                s, t, g = i // 4, (i % 4) // 2, i % 2
                row = NORMS[s][1]
                dve.wait_ge(normT_ready, i + 1)
                if i >= 2:
                    dve.wait_ge(xlo_ready, i - 1)
                nc.vector.tensor_tensor(
                    gained[i % 2][:, :, :], acc[2 * t + g].rearrange("p (k n) -> p k n", k=4),
                    gains[:, 8 * row + 4 * g:8 * row + 4 * g + 4].unsqueeze(2).to_broadcast([P, 4, P]),
                    ALU.mult).then_inc(gained_ready, 1)

            def norm_lo(i):
                s, t, g = i // 4, (i % 4) // 2, i % 2
                xset = NORMS[s][2]
                dve.wait_ge(xhi_ready, i + 1)
                nc.vector.tensor_tensor(xlo[xset][:, 4 * g:4 * g + 4, t * P:t * P + P], gained[i % 2][:, :, :],
                                        xhi[xset][:, 4 * g:4 * g + 4, t * P:t * P + P].bitcast(F32),
                                        ALU.subtract).then_inc(xlo_ready, 1)

            def norm_tile(s, t):
                for i in (4 * s + 2 * t, 4 * s + 2 * t + 1):
                    norm_gain(i)
                for i in (4 * s + 2 * t, 4 * s + 2 * t + 1):
                    norm_lo(i)

            def norm(s):
                norm_gain(4 * s)
                norm_gain(4 * s + 1)
                norm_lo(4 * s)
                norm_gain(4 * s + 2)
                norm_lo(4 * s + 1)
                norm_gain(4 * s + 3)
                norm_lo(4 * s + 2)
                norm_lo(4 * s + 3)

            def update_h(n, scale, tiles=range(T)):
                for t in tiles:
                    dve.wait_ge(halves_done, 2 * n + t + 1)
                    for c in range(2):
                        last = nc.vector.scalar_tensor_tensor(
                            out=h[:, t, 512 * c:512 * c + 512], in0=acc[2 * t + c], scalar=scale,
                            in1=h[:, t, 512 * c:512 * c + 512], op0=ALU.mult, op1=ALU.add)
                    last.then_inc(h_updated, 1)

            def update_and_norm(n, scale, s):
                update_h(n, scale, (0,))
                norm_gain(4 * s)
                norm_gain(4 * s + 1)
                norm_lo(4 * s)
                update_h(n, scale, (1,))
                norm_lo(4 * s + 1)
                norm_gain(4 * s + 2)
                norm_gain(4 * s + 3)
                norm_lo(4 * s + 2)
                norm_lo(4 * s + 3)

            def gate_lo(f, j):
                last_step = isinstance(j, int) and j == STEPS - 1
                hi, lo = (x[:, 0:2, :] for x in ((xhi[X], xlo[X]) if last_step else (gthi, gtlo)))
                dve.wait_ge(gthi_ready, STEPS * f + j + 1)
                nc.vector.tensor_tensor(lo.rearrange("p c n -> p (c n)"), tpb[0],
                                        hi.bitcast(F32).rearrange("p c n -> p (c n)"),
                                        ALU.subtract).then_inc(gtlo_ready, 1)

            def gate(f, st, j, tiles=range(T)):
                for t in tiles:
                    i = 2 * STEPS * f + t + 1
                    dve.wait_ge(th_ready, i + 2 * j)
                    nc.vector.scalar_tensor_tensor(out=half[:, t, :], in0=th[:, t, :], scalar=1.0,
                                                   in1=inb[t][:, 0:256], op0=ALU.add,
                                                   op1=ALU.mult).then_inc(y_ready, 1)
                    dve.wait_ge(y_ready, i + 2 * j)
                    nc.vector.scalar_tensor_tensor(out=gated[:, t, :], in0=inb[t][:, 256:512],
                                                   scalar=rstd_sq_half[:, st, t:t + 1], in1=half[:, t, :],
                                                   op0=ALU.mult, op1=ALU.mult).then_inc(g_ready, 1)

            def ffn(f, st):
                B = S_FFN[f]
                assert following[0] == B + 2
                split_next()
                dve.wait_ge(stats_ready, st + 1)
                for t in range(T):
                    if f in (0, 2):
                        norm_tile(1 if f == 0 else 6, t)
                    gate(f, st, 0, (t,))
                split_next()
                gate_lo(f, 0)
                split_next()
                split_next()
                gate(f, st, 1)
                split_next()
                with dve.Fori(2, STEPS - 1) as j:
                    gate_lo(f, j - 1)
                    split_lo(B + 1, j)
                    split_lo(B + 2, j)
                    gate(f, st, j)
                    split_lo(B + 3, j)
                following[0] += 3 * (STEPS - 3)
                gate_lo(f, STEPS - 2)
                split_next()
                split_next()
                gate(f, st, STEPS - 1)
                gate_lo(f, STEPS - 1)
                split_next()

            def mem_max(l, t):
                dve.wait_ge(ms_ready, 2 * l + t + 1)
                i = 4 * t
                nc.vector.tensor_reduce(mstat[:, 0, i:i + 4],
                                        flat[:, t * 1024:t * 1024 + 1024].rearrange("p (h n) -> p h n", h=4),
                                        AX_X, ALU.max).then_inc(mmax_ready, 1)
                dve.wait_ge(mmax_ready, 2 * l + t + 1)
                nc.vector.tensor_scalar(mstat[:, 1, i:i + 4], mstat[:, 0, i:i + 4], -1.0, None,
                                        ALU.mult).then_inc(mneg_ready, 1)

            def mem_norm(l, t):
                i = 4 * t
                dve.wait_ge(mexp_ready, 8 * l + 4 * t + 4)
                nc.vector.reciprocal(mstat[:, 3, i:i + 4], mstat[:, 2, i:i + 4]).then_inc(mrecip_ready, 1)
                dve.wait_ge(mrecip_ready, 2 * l + t + 1)
                for m in range(MH):
                    last = nc.vector.tensor_scalar(mprob[:, t, m, :], mprob[:, t, m, :],
                                                   mstat[:, 3, i + MEM_AT[m]:i + MEM_AT[m] + 1], None,
                                                   ALU.mult)
                last.then_inc(mprob_ready, 1)

            def mem_out_lo(l):
                dve.wait_ge(mohi_ready, l + 1)
                nc.vector.tensor_tensor(xlo[Y][:, 6:8, :].rearrange("p c n -> p (c n)"), tpb[0],
                                        xhi[Y][:, 6:8, :].bitcast(F32).rearrange("p c n -> p (c n)"),
                                        ALU.subtract).then_inc(molo_ready, 1)

            dve.wait_ge(gainsT_ready, 1)
            nc.vector.tensor_copy(gains[:], tpb[0][:, 0:72]).then_inc(gains_ready, 1)
            dve.wait_ge(gains_ready, 1)
            norm_gain(0)
            norm_gain(1)
            norm_lo(0)
            split_next()
            norm_lo(1)
            norm_gain(2)
            norm_gain(3)
            norm_lo(2)
            norm_lo(3)
            split_next()
            ffn(0, ST_X)

            update_h(S_FFN0 + FFN_UNITS - 1, 0.5)
            split_next()
            norm(2)
            split_next()
            split_next()
            split_next()
            split_next()
            norm(3)
            split_next()
            dve.wait_ge(glT_ready, 1)
            dve.wait_ge(pair_ready, 1)
            nc.vector.tensor_copy(glT, tpb[0][0:RANK, 0:256]).then_inc(glT_taken, 1)
            split_next()
            split_next()
            split_next()
            for t in range(T):
                dve.wait_ge(gate_ready, t + 1)
                nc.vector.tensor_scalar(gmin[:, t, :], tpb[t][:, 0:GH * DK], 0.0, None,
                                        ALU.min).then_inc(gmin_ready, 1)
                dve.wait_ge(gmin_ready, t + 1)
                nc.vector.scalar_tensor_tensor(out=gneg[:, t, :], in0=gmin[:, t, :], scalar=2.0,
                                               in1=tpb[t][:, 0:GH * DK], op0=ALU.mult,
                                               op1=ALU.subtract).then_inc(gneg_ready, 1)
            for t in range(T):
                dve.wait_ge(gln_ready, t + 1)
                nc.vector.tensor_tensor(loga[:, t, :], gmin[:, t, :], gneg[:, t, :],
                                        ALU.subtract).then_inc(loga_ready, 1)
            split_next()
            split_next()

            def take_scores(n):
                dve.wait_ge(score_ready, n + 1)
                if n == NLEV:
                    nc.vector.tensor_copy(cross[:, :, :].rearrange("p h n -> p (h n)"),
                                          flat[:, 1024:1536]).then_inc(score_taken, 1)
                    return
                if n:
                    dve.wait_ge(score_taken, n)
                nc.vector.copy_predicated(
                    scores.rearrange("p (i n) -> p i n", n=P),
                    pair[:, n * P:n * P + P].unsqueeze(1).to_broadcast([P, GH * T, P]),
                    flat[:, 1024:2048].rearrange("p (i n) -> p i n", n=P)).then_inc(score_taken, 1)

            def join(n):
                b = 1 << n
                dve.wait_ge(decay_ready, n + 1)
                if n >= 2:
                    dve.wait_ge(score_ready, n)
                for s, src in ((0, kT), (1, qT)):
                    pick_half = lambda ap: ap.rearrange("p (m s b) -> p m s b", s=2, b=b)[:, :, s, :]
                    last = nc.vector.tensor_tensor(pick_half(joined[n % 2][:, :]), pick_half(decay[n % 2]),
                                                   pick_half(src), ALU.mult)
                last.then_inc(joined_ready, 1)

            dve.wait_ge(scores_zero, 1)
            dve.wait_ge(qkT_taken, 4)
            join(0)
            split_next()
            for n in range(NLEV):
                if n >= 1:
                    join(n)
                if n < NLEV - 1:
                    take_scores(n)
                    split_next() if n < 6 else None
            take_scores(NLEV - 1)
            mem_max(0, 0)
            take_scores(NLEV)
            mem_max(0, 1)
            dve.wait_ge(rth_ready, 1)
            nc.vector.scalar_tensor_tensor(out=sgate[:, :, :], in0=sgate[:, :, :], scalar=1.0, in1=r_gla,
                                           op0=ALU.add, op1=ALU.mult).then_inc(rsilu_ready, 1)
            dve.wait_ge(rsilu_ready, 1)
            for t in range(T):
                v = sgate[:, t, :].rearrange("p (h n) -> p h n", h=GH)
                last = nc.vector.scalar_tensor_tensor(
                    out=v, in0=v, scalar=0.5, in1=ghead[:, :].unsqueeze(1).to_broadcast([P, GH, DV]),
                    op0=ALU.mult, op1=ALU.mult)
            last.then_inc(sgate_ready, 1)
            for t in range(T):
                mem_norm(0, t)
                dve.wait_ge(orstd_ready, t + 1)
                if t == 0:
                    dve.wait_ge(sgate_ready, 1)
                for hh in range(GH):
                    at = gla_at(t, hh)
                    last = nc.vector.scalar_tensor_tensor(
                        out=ohead[:, t, hh * DV:hh * DV + DV], in0=flat[:, at:at + DV],
                        scalar=ostat[:, 2, GH * t + hh:GH * t + hh + 1],
                        in1=sgate[:, t, hh * DV:hh * DV + DV], op0=ALU.mult, op1=ALU.mult)
                last.then_inc(ohead_ready, 1)
            for i in range(4):
                t, g = i // 2, i % 2
                k = 4 if g == 0 else 2
                dve.wait_ge(oThi_ready, i + 1)
                nc.vector.tensor_tensor(xlo[Y][:, 4 * g:4 * g + k, t * P:t * P + P],
                                        tpb[g][:, 0:k * P].rearrange("p (k n) -> p k n", k=k),
                                        xhi[Y][:, 4 * g:4 * g + k, t * P:t * P + P].bitcast(F32),
                                        ALU.subtract).then_inc(oTlo_ready, 1)
            mem_out_lo(0)
            split_next()
            split_next()
            update_and_norm(S_WO0 + 3, 1.0, 4)
            split_next()
            ffn(1, ST_H + 1)

            update_and_norm(S_FFN1 + FFN_UNITS - 1, 0.5, 5)
            split_next()
            ffn(2, ST_H + 2)

            update_h(S_FFN2 + FFN_UNITS - 1, 0.5)
            split_next()
            split_next()
            norm(7)
            for _ in range(4):
                split_next()
            for t in range(T):
                dve.wait_ge(halves_done, 2 * S_FG + t + 1)
                nc.vector.scalar_tensor_tensor(out=fg[:, 0, t, :], in0=inb[t][:, 0:FH],
                                               scalar=rstd[:, ST_H + 2, t:t + 1], in1=bf[:], op0=ALU.mult,
                                               op1=ALU.add).then_inc(fg_logit, 1)
                dve.wait_ge(fg_logit, t + 1)
                nc.vector.tensor_scalar(fg[:, 3, t, :], fg[:, 0, t, :], 0.0, None, ALU.min).then_inc(chunk_taken, 1)
            dve.wait_ge(chunk_taken, 22)
            nc.vector.scalar_tensor_tensor(out=fg[:, 1], in0=fg[:, 3], scalar=2.0, in1=fg[:, 0], op0=ALU.mult,
                                           op1=ALU.subtract).then_inc(fg_neg, 1)
            dve.wait_ge(fg_ln, 1)
            nc.vector.tensor_tensor(fg[:, 3], fg[:, 3], fg[:, 1], ALU.subtract).then_inc(fg_log, 1)
            split_next()
            split_next()
            dve.wait_ge(cum_ready, 1)
            nc.vector.tensor_scalar(negD[:], tpb[0][0:FH, 0:256], -1.0, None, ALU.mult).then_inc(cum_taken, 1)
            dve.wait_ge(cum_ready, 2)
            nc.vector.tensor_copy(Dtok[:, :, :], tpb[1][:, 0:16].rearrange("p (t n) -> p t n", t=2)[:, :, 0:FH]
                                  ).then_inc(cum_taken, 1)
            dve.wait_ge(cum_taken, 2)
            split_next()
            split_next()
            split_next()
            split_next()
            for n, t in enumerate((1, 0)):
                dve.wait_ge(fs_ready, n + 1)
                p = fprob1 if t else fprob0
                wide = P * (t + 1)
                mask = causal[:, :] if t else causal[:, P:2 * P]
                for hh in range(FH):
                    at = fox_at(t, hh)
                    last = nc.vector.scalar_tensor_tensor(out=p[:, hh, :], in0=flat[:, at:at + wide],
                                                          scalar=Dtok[:, t, hh:hh + 1], in1=mask, op0=ALU.add,
                                                          op1=ALU.add)
                last.then_inc(flogit_ready, 1)
                dve.wait_ge(flogit_ready, n + 1)
                i = FH * t
                nc.vector.tensor_reduce(fstat[:, 0, i:i + FH], p[:, :, :], AX_X, ALU.max).then_inc(fmax_ready, 1)
                dve.wait_ge(fmax_ready, n + 1)
                nc.vector.tensor_scalar(fstat[:, 1, i:i + FH], fstat[:, 0, i:i + FH], -1.0, None,
                                        ALU.mult).then_inc(fneg_ready, 1)
            mem_max(1, 0)
            for n, t in enumerate((1, 0)):
                dve.wait_ge(fexp_ready, FH * (n + 1))
                p = fprob1 if t else fprob0
                i = FH * t
                nc.vector.reciprocal(fstat[:, 3, i:i + FH], fstat[:, 2, i:i + FH]).then_inc(frecip_ready, 1)
                dve.wait_ge(frecip_ready, n + 1)
                for hh in range(FH):
                    last = nc.vector.tensor_scalar(p[:, hh, :], p[:, hh, :], fstat[:, 3, i + hh:i + hh + 1], None,
                                                   ALU.mult)
                last.then_inc(fprob_ready, 1)
                if t == 1:
                    mem_max(1, 1)
            split_next()
            mem_norm(1, 0)
            mem_norm(1, 1)
            for c in range(3):
                dve.wait_ge(fohi_ready, c + 1)
                nc.vector.tensor_tensor(xlo[Y][:, 2 * c:2 * c + 2, :].rearrange("p c n -> p (c n)"), acc[c],
                                        xhi[Y][:, 2 * c:2 * c + 2, :].bitcast(F32).rearrange("p c n -> p (c n)"),
                                        ALU.subtract).then_inc(folo_ready, 1)
            mem_out_lo(1)
            split_next()
            split_next()
            update_and_norm(S_WO1 + 3, 1.0, 8)
            split_next()
            ffn(3, ST_H + 4)

            dve.wait_ge(final_landed, 16)
            for t in range(T):
                update_h(S_FFN3 + FFN_UNITS - 1, 0.5, (t,))
                dve.wait_ge(rstd_ready, ST_H + 5 + t + 1)
                for c in range(2):
                    cols = slice(512 * c, 512 * c + 512)
                    nc.vector.scalar_tensor_tensor(out=h[:, t, cols], in0=h[:, t, cols],
                                                   scalar=rstd[:, ST_H + 5, t:t + 1], in1=gfinal[:, cols],
                                                   op0=ALU.mult, op1=ALU.mult).then_inc(out_ready, 1)


def gla_at(t, h):
    return (4 if t == 0 else 0) * 512 + (h // 2) * 512 + (h % 2) * DV


def fox_at(t, h):
    if t == 1:
        return h * 256
    return 3 * 512 + h * P if h < 4 else 7 * 512 + (h - 4) * P


H_UPDATES_BEFORE = {2: 1, 4: 2, 5: 3, 6: 3, 7: 4, 8: 5}


_INS = ["x", "mem", "norm_ffn", "w_ffn_in", "w_ffn_out", "norm_mix", "norm_mem", "w_mem_kv", "w_out", "w_in_a",
        "w_gate_up", "b_gate", "norm_gla_head", "w_in_b", "norm_shared", "w_kv_shared", "w_fgate", "b_fgate",
        "norm_final"]


def kernel(**inputs):
    import concourse.bacc as _bacc
    from concourse.bass_utils import run_bass_kernel_spmd as _run

    nc = _bacc.Bacc("TRN2", target_bir_lowering=False, num_devices=1)
    arrays, args = {}, {}
    host = {n: np.ascontiguousarray(inputs[n]) for n in _INS}
    host.update(shape_constants())
    for name, v in host.items():
        arrays[f"in_{name}_dram"] = v
        args[name] = nc.dram_tensor(f"in_{name}_dram", v.shape, mybir.dt.from_np(v.dtype),
                                    kind="ExternalInput").ap()
    out = nc.dram_tensor("out_0_dram", (1, T * P, D), F32, kind="ExternalOutput").ap()
    build(nc, args, out)
    r = _run(nc, [arrays], core_ids=[0])
    return r.results[0]["out_0_dram"]
```

```python
from contextlib import ExitStack

import numpy as np

import concourse.bass as bass
from concourse import mybir

F32 = mybir.dt.float32
F32R = mybir.dt.float32r
U8 = mybir.dt.uint8
ALU = mybir.AluOpType
ACT = mybir.ActivationFunctionType
AX_X = mybir.AxisListType.X

P = 128
T = 2
D = 1024
KT = D // P
FF = 2816
STEPS = FF // 256
GH, DK, DV = 4, 96, 192
RANK = 16
FH, FD = 6, 128
MH, MD = 4, 64
OUT_ORDER = (6, 0, 2, 4)
MEM_AT = [0, 2, 1, 3]
EPS = 1e-6
NLEV = 8
MASKED = -1.0e30
WORK = 16160
RING = 3

A_CHUNKS = [(2304, 272), (0, 512), (512, 512), (1024, 512), (1536, 384), (1920, 384)]

FFN_UNITS = 3 * STEPS
S_FFN0 = 0
S_MK0 = S_FFN0 + FFN_UNITS
S_PA = [S_MK0 + 2, S_MK0 + 4, S_MK0 + 6] + [S_MK0 + 10 + 2 * c for c in range(3)]
S_MK1 = S_PA[2] + 2
S_WO0 = S_PA[-1] + 2
S_FFN1 = S_WO0 + 4
S_FFN2 = S_FFN1 + FFN_UNITS
S_KV = [S_FFN2 + FFN_UNITS + at for at in (0, 4, 9)]
S_PB = [S_FFN2 + FFN_UNITS + at for at in (2, 7)]
S_FG = S_KV[1] + 2
B_CHUNKS = [512, 0]
FOX_T = [0, 1, 5, 2, 3, 4]
S_WO1 = S_KV[2] + 2
S_FFN3 = S_WO1 + 4
S_END = S_FFN3 + FFN_UNITS
S_FFN = [S_FFN0, S_FFN1, S_FFN2, S_FFN3]
S_MK = [S_MK0, S_MK1]
S_WO = [S_WO0, S_WO1]

X, Y = 0, 1
NORMS = [("x", 0, X), ("mem", 6, Y), ("h", 4, X), ("mem", 7, Y), ("h", 1, X),
         ("h", 2, X), ("h", 8, Y), ("h", 5, X), ("h", 3, X)]
ST_X, ST_MEM, ST_H = 0, 1, 2


def shape_constants():
    i = np.arange(P)
    ident = np.eye(P, dtype=np.float32)
    upper = (i[:, None] <= i[None, :]).astype(np.float32)
    upper_ones = np.concatenate([upper, np.ones((P, P), np.float32)], 1)
    between = np.zeros((P, NLEV + 1, P), np.float32)
    pair = np.zeros((P, NLEV, P), np.float32)
    pair[:, 0] = ident
    for n in range(NLEV - 1):
        b = 1 << n
        mid = (i // (2 * b)) * 2 * b + b
        late = i >= mid
        s = i[:, None]
        between[:, n] = np.where(late, (s >= mid) & (s <= i), (s > i) & (s < mid))
        same = (i[:, None] // (2 * b)) == (i[None, :] // (2 * b))
        pair[:, n + 1] = same & ~late[:, None] & late[None, :]
    between[:, NLEV - 1] = i[:, None] > i[None, :]
    between[:, NLEV] = upper
    between /= 16.0
    causal = np.zeros((P, 2 * P), np.float32)
    causal[:, P:] = np.where(i[None, :] <= i[:, None], 0.0, MASKED)
    pick = np.zeros((FH, FH, P), np.float32)
    for h in range(FH):
        pick[h, h] = 1.0
    return {"c_ident": ident, "c_upper": upper_ones, "c_between": between.reshape(P, -1),
            "c_pair": pair.reshape(P, -1), "c_causal": causal, "c_pick": pick.reshape(FH, -1)}


def build(nc, a, out):
    with ExitStack() as ctx:
        def sb(name, shape, dt=F32):
            return ctx.enter_context(nc.sbuf_tensor(name, shape, dt))

        def sem(name):
            return ctx.enter_context(nc.semaphore(name))

        banks = ctx.enter_context(nc.psum_tensor("banks", [P, 8, 512], F32))
        acc = [banks[:, i, :] for i in range(4)]
        inb = [banks[:, 4 + i, :] for i in range(2)]
        tpb = [banks[:, 6 + i, :] for i in range(2)]
        flat = banks[:, :, :].rearrange("p b n -> p (b n)")
        fo_bank = [inb[0], inb[1], tpb[1]]

        raw = [sb(f"raw{i}", [P, 2048]) for i in range(RING)]
        whi = [sb(f"whi{i}", [P, 2048], F32R) for i in range(RING)]
        wlo = [sb(f"wlo{i}", [P, 2048], F32R) for i in range(RING)]
        xhi = [sb(f"xhi{i}", [P, KT, 256], F32R) for i in range(2)]
        xlo = [sb(f"xlo{i}", [P, KT, 256], F32R) for i in range(2)]
        gained = [sb(f"gained{i}", [P, 4, P]) for i in range(2)]
        h = sb("h", [P, T, D])
        gthi = sb("gthi", [P, 2, 256], F32R)
        gtlo = sb("gtlo", [P, 2, 256], F32R)
        squares = sb("squares", [P, 8, T])
        meansq = sb("meansq", [P, 8, T])
        rstd = sb("rstd", [P, 8, T])
        rstd_half = sb("rstd_half", [P, 8, T])
        rstd_sq_half = sb("rstd_sq_half", [P, 8, T])
        power = sb("power", [P, 8])
        ident = sb("ident", [P, P])
        upper = sb("upper", [P, 2 * P])
        gains_raw = sb("gains_raw", [72, P])
        gains = sb("gains", [P, 72])
        work = sb("work", [P, WORK])
        ghead = sb("ghead", [P, DV])
        memkv_l = [sb(f"memkv{l}", [P, T, 512]) for l in range(2)]
        mstat = sb("mstat", [P, 4, 16])

        cursor = [0]

        def carve(n, parts=P):
            s = cursor[0]
            cursor[0] += n
            assert cursor[0] <= WORK, cursor[0]
            return work[0:parts, s:s + n]

        mem = work[:, 0:T * D].rearrange("p (t n) -> p t n", t=T)
        th, half, gated = (work[:, WORK - 512 * (i + 1):WORK - 512 * i].rearrange("p (t n) -> p t n", t=T)
                           for i in range(3))
        pair_f32 = work[:, T * D:T * D + NLEV * P]
        scratch = work[:, WORK - D:WORK]
        gfinal = work[:, 0:D]

        mkT = carve(512).rearrange("p (a n) -> p a n", a=2)
        mqT = carve(512).rearrange("p (a n) -> p a n", a=2)
        mprob_flat, mprobT_flat = carve(2048), carve(2048)
        mprob = mprob_flat.rearrange("p (t h n) -> p t h n", t=2, h=4)
        mprobT = mprobT_flat.rearrange("p (k h n) -> p k h n", k=2, h=4)
        after_memory = cursor[0]
        pa = carve(T * 1552).rearrange("p (t n) -> p t n", t=T)
        v_gla = pa[:, :, 0:768]
        r_gla = pa[:, :, 768:1536]
        glow = pa[:, :, 1536:1552]
        qk_flat = carve(T * 1024)
        qk = qk_flat.rearrange("p (t n) -> p t n", t=T)
        qT = carve(1024, DK)
        kT = carve(1024, DK)
        gates = carve(2304)
        gmin, gneg, loga = (gates[:, 768 * i:768 * i + 768].rearrange("p (t n) -> p t n", t=T) for i in range(3))
        scores = carve(1024)
        cross = carve(512).rearrange("p (h n) -> p h n", h=GH)
        glT = mprob_flat[0:RANK, 0:256]
        joined = [mprob_flat[0:DK, 1024 * i:1024 * i + 1024] for i in range(2)]
        decay = [mprobT_flat[0:DK, 1024 * i:1024 * i + 1024] for i in range(2)]
        osquares = mprobT_flat[:, 0:T * GH * DV]
        sgate = qk_flat[:, 0:1536].rearrange("p (t n) -> p t n", t=T)
        ohead = gates[:, 0:1536].rearrange("p (t n) -> p t n", t=T)
        cursor[0] = after_memory
        kv = carve(T * 1536).rearrange("p (t n) -> p t n", t=T)
        qb_flat = carve(T * 1024)
        qb = qb_flat.rearrange("p (t n) -> p t n", t=T)
        fkT_flat = carve(1536)
        fkT = fkT_flat.rearrange("p (h n) -> p h n", h=FH)
        fqT = carve(1536).rearrange("p (h n) -> p h n", h=FH)
        fprob0 = carve(768).rearrange("p (h n) -> p h n", h=FH)
        fprob1 = carve(1536).rearrange("p (h n) -> p h n", h=FH)
        fprobT0 = qb_flat[:, 0:1536].rearrange("p (h n) -> p h n", h=FH)
        fprobT1 = fkT_flat[:, 0:768].rearrange("p (h n) -> p h n", h=FH)

        between = sb("between", [P, (NLEV + 1) * P])
        pair = sb("pair", [P, NLEV * P], U8)
        causal = sb("causal", [P, 2 * P])
        pick_rows = sb("pick_rows", [33, FH * P])
        pick, ones_row = pick_rows[0:FH, :], pick_rows[32:33, 0:P]
        gate_rows = sb("gate_rows", [33, GH * DK])
        wgate, bgate = gate_rows[0:RANK, :], gate_rows[32:33, :]
        bf = sb("bf", [P, FH])
        fg = sb("fg", [P, 4, T, FH])
        negD = sb("negD", [FH, 256])
        Dtok = sb("Dtok", [P, T, FH])
        fstat = sb("fstat", [P, 4, T * FH])
        ostat = sb("ostat", [P, 3, T * GH])

        raw_landed = [sem(f"raw_landed{i}") for i in range(RING)]
        hi_ready = sem("hi_ready")
        lo_ready = sem("lo_ready")
        halves_done = sem("halves_done")
        x_landed = [sem(f"x_landed{t}") for t in range(T)]
        mem_landed = sem("mem_landed")
        ident_landed = sem("ident_landed")
        gains_landed = sem("gains_landed")
        const_landed = sem("const_landed")
        final_landed = sem("final_landed")
        gainsT_ready = sem("gainsT_ready")
        gains_ready = sem("gains_ready")
        normT_ready = sem("normT_ready")
        gained_ready = sem("gained_ready")
        xhi_ready = sem("xhi_ready")
        xlo_ready = sem("xlo_ready")
        squares_ready = sem("squares_ready")
        meansq_ready = sem("meansq_ready")
        rstd_ready = sem("rstd_ready")
        half_ready = sem("half_ready")
        stats_ready = sem("stats_ready")
        power_set = sem("power_set")
        ones_set = sem("ones_set")
        th_ready = sem("th_ready")
        y_ready = sem("y_ready")
        g_ready = sem("g_ready")
        gT_ready = sem("gT_ready")
        gthi_ready = sem("gthi_ready")
        gtlo_ready = sem("gtlo_ready")
        chunk_taken = sem("chunk_taken")
        h_updated = sem("h_updated")
        glT_ready, glT_taken = sem("glT_ready"), sem("glT_taken")
        gate_product = sem("gate_product")
        pair_ready = sem("pair_ready")
        gate_ready, gmin_ready, gneg_ready = sem("gate_ready"), sem("gmin_ready"), sem("gneg_ready")
        gexp_ready, gln_ready, loga_ready = sem("gexp_ready"), sem("gln_ready"), sem("loga_ready")
        qkT_ready, qkT_taken = sem("qkT_ready"), sem("qkT_taken")
        span_ready, decay_ready = sem("span_ready"), sem("decay_ready")
        joined_ready, score_ready, score_taken = sem("joined_ready"), sem("score_ready"), sem("score_taken")
        scores_zero = sem("scores_zero")
        o_ready, osq_ready, omean_ready, orstd_ready = (sem("o_ready"), sem("osq_ready"),
                                                        sem("omean_ready"), sem("orstd_ready"))
        rth_ready, rsilu_ready, sgate_ready, ohead_ready = (sem("rth_ready"), sem("rsilu_ready"),
                                                            sem("sgate_ready"), sem("ohead_ready"))
        oT_ready, oThi_ready, oTlo_ready = sem("oT_ready"), sem("oThi_ready"), sem("oTlo_ready")
        mT_ready, mT_taken = sem("mT_ready"), sem("mT_taken")
        ms_ready, mmax_ready, mneg_ready = sem("ms_ready"), sem("mmax_ready"), sem("mneg_ready")
        mexp_ready, mrecip_ready, mprob_ready = sem("mexp_ready"), sem("mrecip_ready"), sem("mprob_ready")
        mpT_ready, mpT_taken = sem("mpT_ready"), sem("mpT_taken")
        mo_ready, mohi_ready, molo_ready = sem("mo_ready"), sem("mohi_ready"), sem("molo_ready")
        fg_logit, fg_min, fg_neg, fg_exp, fg_ln, fg_log = (sem("fg_logit"), sem("fg_min"), sem("fg_neg"),
                                                          sem("fg_exp"), sem("fg_ln"), sem("fg_log"))
        cum_ready, cum_taken = sem("cum_ready"), sem("cum_taken")
        fT_ready, fT_taken = sem("fT_ready"), sem("fT_taken")
        fs_ready, flogit_ready, fmax_ready, fneg_ready = (sem("fs_ready"), sem("flogit_ready"),
                                                          sem("fmax_ready"), sem("fneg_ready"))
        fexp_ready, frecip_ready, fprob_ready = sem("fexp_ready"), sem("frecip_ready"), sem("fprob_ready")
        fpT_ready, fpT_taken = sem("fpT_ready"), sem("fpT_taken")
        fo_ready, fohi_ready, folo_ready = sem("fo_ready"), sem("fohi_ready"), sem("folo_ready")
        out_ready, out_stored = sem("out_ready"), sem("out_stored")

        def rows(w):
            return w.rearrange("(k p) n -> p k n", p=P)

        units = {}
        for l in range(2):
            for u in range(2):
                units[S_MK[l] + u] = (rows(a["w_mem_kv"][l])[:, 4 * u:4 * u + 4, :], 4, 512)
            for u, k in enumerate(OUT_ORDER):
                units[S_WO[l] + u] = (rows(a["w_out"][l])[:, k:k + 2, :], 2, D)
        for c, (at, wide) in enumerate(A_CHUNKS):
            for u in range(2):
                units[S_PA[c] + u] = (rows(a["w_in_a"][0])[:, 4 * u:4 * u + 4, at:at + wide], 4, wide)
        for c in range(3):
            for u in range(2):
                units[S_KV[c] + u] = (rows(a["w_kv_shared"])[:, 4 * u:4 * u + 4, 512 * c:512 * c + 512], 4, 512)
        units[S_FG] = (rows(a["w_fgate"]), KT, FH)
        for c, at in enumerate(B_CHUNKS):
            for u in range(2):
                units[S_PB[c] + u] = (rows(a["w_in_b"][0])[:, 4 * u:4 * u + 4, at:at + 512], 4, 512)

        def size(n):
            return units[n][1] * units[n][2] if n in units else 2048

        def slot_view(ring, n):
            _, k, wide = units[n]
            return ring[n % RING][:, 0:k * wide].rearrange("p (k n) -> p k n", k=k)

        ffn_in = [a["w_ffn_in"][f // 2, f % 2].rearrange("(k p) (s n) -> p k s n", p=P, s=2) for f in range(4)]
        ffn_out = [a["w_ffn_out"][f // 2, f % 2].rearrange("(j k p) n -> j p k n", p=P, k=2) for f in range(4)]

        block = ctx.enter_context(nc.Block())

        @block.sync
        def _(sp):
            def load(dst, src, signal):
                sp.dma_start(dst, src).then_inc(signal, 16)

            def claim(base, j=0):
                if not isinstance(j, int) or base >= RING:
                    sp.wait_ge(lo_ready, base + 3 * j - RING + 1)

            def load_in(f, u, base, step, j=0):
                claim(base, j)
                dst = raw[base % RING][:, :].rearrange("p (k s n) -> p k s n", k=4, s=2)
                col = step * 256
                for s in range(2):
                    sp.dma_start(dst[:, :, s, :], ffn_in[f][:, 4 * u:4 * u + 4, s, bass.ds(col, 256)]).then_inc(
                        raw_landed[base % RING], 16)

            def load_out(f, base, step, j=0):
                claim(base, j)
                dst = raw[base % RING][:, :].rearrange("p (k n) -> p k n", k=2)
                src = ffn_out[f][bass.ds(step, 1)].rearrange("a p k n -> p (a k) n")
                load(dst, src, raw_landed[base % RING])

            def load_unit(n):
                claim(n)
                load(slot_view(raw, n), units[n][0], raw_landed[n % RING])

            def load_ffn(f):
                B = S_FFN[f]
                load_in(f, 0, B, 0)
                load_in(f, 1, B + 1, 0)
                load_in(f, 0, B + 2, 1)
                load_in(f, 1, B + 3, 1)
                load_out(f, B + 4, 0)
                with sp.Fori(2, STEPS) as j:
                    load_in(f, 0, B - 1, j, j)
                    load_in(f, 1, B, j, j)
                    load_out(f, B + 1, j - 1, j)
                load_out(f, B + FFN_UNITS - 1, STEPS - 1)

            mixer_consts = [(upper[:], a["c_upper"]), (between[:], a["c_between"]), (pair_f32, a["c_pair"]),
                            (causal[:], a["c_causal"]), (pick, a["c_pick"]), (wgate, a["w_gate_up"][0]),
                            (bgate, a["b_gate"]),
                            (ghead[:], a["norm_gla_head"][0:1, :].to_broadcast([P, DV])),
                            (bf[:], a["b_fgate"].rearrange("(a n) -> a n", a=1).to_broadcast([P, FH]))]
            B = S_FFN[0]
            xr = a["x"][0].rearrange("(t p) d -> p t d", p=P)
            load(h[:, 0, :], xr[:, 0, :], x_landed[0])
            load(ident[:], a["c_ident"], ident_landed)
            load_in(0, 0, B, 0)
            load(h[:, 1, :], xr[:, 1, :], x_landed[1])
            load_in(0, 1, B + 1, 0)
            load(mem[:, :, :], a["mem"][0].rearrange("(t p) d -> p t d", p=P), mem_landed)
            load_in(0, 0, B + 2, 1)
            load_in(0, 1, B + 3, 1)
            load_out(0, B + 4, 0)
            with sp.Fori(2, STEPS) as j:
                load_in(0, 0, B - 1, j, j)
                load_in(0, 1, B, j, j)
                load_out(0, B + 1, j - 1, j)
            for dst, src in mixer_consts:
                load(dst, src, const_landed)
            load_out(0, B + FFN_UNITS - 1, STEPS - 1)
            for n in range(S_MK0, S_FFN1):
                load_unit(n)
            load_ffn(1)
            load_ffn(2)
            for n in range(S_KV[0], S_FFN3):
                load_unit(n)
            load_ffn(3)
            sp.wait_ge(folo_ready, 3)
            sp.wait_ge(molo_ready, 2)
            sp.dma_start(gfinal, a["norm_final"].rearrange("(a n) -> a n", a=1).to_broadcast([P, D])).then_inc(
                final_landed, 16)
            for t in range(T):
                for c in range(2):
                    cols = slice(512 * c, 512 * c + 512)
                    sp.wait_ge(out_ready, 2 * t + c + 1)
                    sp.dma_start(out[0].rearrange("(t p) d -> t p d", p=P)[t][:, cols],
                                 h[:, t, cols]).then_inc(out_stored, 16)
            sp.wait_ge(out_stored, 16 * 2 * T)

        def landed(n):
            total = 0
            for m in range(n % RING, n + 1, RING):
                total += 32 if is_input(m) else 16
            return total

        def is_input(n):
            for B in S_FFN:
                if B <= n < B + FFN_UNITS:
                    r = n - B
                    return r != FFN_UNITS - 1 and (r < 2 or r % 3 != 1)
            return False

        @block.tensor
        def _(pe):
            def split_matmul(dst, lh, ll, rh, rl, start, stop):
                nc.tensor.matmul(dst, lh, rh, start=start, stop=False)
                nc.tensor.matmul(dst, lh, rl, start=False, stop=False)
                return nc.tensor.matmul(dst, ll, rh, start=False, stop=stop)

            def norm_transposes(s, tiles=range(T), groups=range(2)):
                src, _, _ = NORMS[s]
                rows_of = mem if src == "mem" else h
                for t in tiles:
                    if src == "x":
                        pe.wait_ge(x_landed[t], 16)
                    elif src == "mem":
                        pe.wait_ge(mem_landed, 16)
                    for g in groups:
                        if src == "h":
                            pe.wait_ge(h_updated, 4 * H_UPDATES_BEFORE[s] - 3 + 2 * t + g)
                        i = 4 * s + 2 * t + g
                        if i >= 4:
                            pe.wait_ge(gained_ready, i - 3)
                        for k in range(4):
                            last = nc.tensor.transpose(acc[2 * t + g][:, k * P:k * P + P],
                                                       rows_of[:, t, (4 * g + k) * P:(4 * g + k + 1) * P], ident[:])
                        last.then_inc(normT_ready, 1)

            def proj_unit(n, xset, k0, chunk_start, chunk_end, s, j=0, bank_free=None, hooks=None):
                if n in units and isinstance(j, int):
                    _, kn, wide = units[n]
                else:
                    kn, wide = 4, 512
                hi_v = whi[n % RING][:, 0:kn * wide].rearrange("p (k n) -> p k n", k=kn)
                lo_v = wlo[n % RING][:, 0:kn * wide].rearrange("p (k n) -> p k n", k=kn)
                pe.wait_ge(lo_ready, n + 3 * j + 1)
                for t in range(T):
                    if bank_free:
                        bank_free(t)
                    if s is not None:
                        pe.wait_ge(xlo_ready, 4 * s + 2 * t + (k0 + kn) // 4)
                    for k in range(kn):
                        if hooks and (t, k) in hooks:
                            hooks[t, k]()
                        c = k0 + k
                        last = split_matmul(inb[t][:, 0:wide], xhi[xset][:, c, t * P:t * P + P],
                                            xlo[xset][:, c, t * P:t * P + P], hi_v[:, k, :], lo_v[:, k, :],
                                            chunk_start and k == 0, chunk_end and k == kn - 1)
                    last.then_inc(halves_done, 1)

            def out_unit(n, lh, ll, first, final, j=0, hooks=None):
                hi_v = whi[n % RING][:, :].rearrange("p (k n) -> p k n", k=2)
                lo_v = wlo[n % RING][:, :].rearrange("p (k n) -> p k n", k=2)
                pe.wait_ge(lo_ready, n + 3 * j + 1)
                for t in range(T):
                    for k in range(2):
                        if hooks and (t, k) in hooks:
                            hooks[t, k]()
                        for c in range(2):
                            last = split_matmul(acc[2 * t + c], lh[:, k, t * P:t * P + P], ll[:, k, t * P:t * P + P],
                                                hi_v[:, k, 512 * c:512 * c + 512], lo_v[:, k, 512 * c:512 * c + 512],
                                                first and k == 0, final and k == 1)
                    last.then_inc(halves_done, 1)

            def mixed(k):
                return (gthi, gtlo) if k == 6 else (xhi[Y][:, k:k + 2, :], xlo[Y][:, k:k + 2, :])

            def gate_transposes(f, j):
                pe.wait_ge(g_ready, 2 * (STEPS * f) + 2 * j + 2)
                for c in range(2):
                    for t in range(T):
                        last = nc.tensor.transpose(tpb[0][:, c * 256 + t * P:c * 256 + t * P + P],
                                                   gated[:, t, c * P:c * P + P], ident[:])
                last.then_inc(gT_ready, 1)

            def ffn(f, s):
                B = S_FFN[f]

                def into(base, j=0):
                    proj_unit(base, X, 0, True, False, None, j)
                    proj_unit(base + 1, X, 4, False, True, None, j)

                def outof(base, step, j, first=False):
                    pe.wait_ge(gtlo_ready, STEPS * f + step + 1)
                    out_unit(base, gthi, gtlo, first, False, j)

                hooks = {(0, 1 + 2 * g): lambda g=g: norm_transposes(s, (1,), (g,)) for g in range(2)}
                if f == 0:
                    hooks = {(1, 2): lambda: norm_transposes(1, (0,))}
                proj_unit(B, X, 0, True, False, s, hooks=hooks)
                if f == 0:
                    norm_transposes(1, (1,))
                proj_unit(B + 1, X, 4, False, True, s)
                proj_unit(B + 2, X, 0, True, False, None, bank_free=lambda t: pe.wait_ge(
                    g_ready, 2 * (STEPS * f) + t + 1))
                gate_transposes(f, 0)
                proj_unit(B + 3, X, 4, False, True, None)
                pe.wait_ge(gained_ready, 4 * (s + 1 + (f in (0, 2))))
                outof(B + 4, 0, 0, first=True)
                gate_transposes(f, 1)
                with pe.Fori(2, STEPS - 1) as j:
                    into(B - 1, j)
                    outof(B + 1, j - 1, j)
                    gate_transposes(f, j)
                into(B + FFN_UNITS - 4)
                pe.wait_ge(gtlo_ready, STEPS * f + STEPS - 1)
                out_unit(B + FFN_UNITS - 2, gthi, gtlo, False, False,
                         hooks={(1, 0): lambda: gate_transposes(f, STEPS - 1)})
                pe.wait_ge(gtlo_ready, STEPS * f + STEPS)
                out_unit(B + FFN_UNITS - 1, xhi[X][:, 0:2, :], xlo[X][:, 0:2, :], False, True,
                         hooks={(1, 1): lambda: norm_transposes(5, (0,))} if f == 1 else None)

            def chunk_free(c, t=1):
                pe.wait_ge(chunk_taken, 2 * c - 1 + t)

            def mem_operands(l):
                for i, (src, at) in enumerate([(memkv_l[l], 0), (qk if l == 0 else qb, 768)]):
                    for c in range(2):
                        for t in range(T):
                            last = nc.tensor.transpose(tpb[i][:, c * 256 + t * P:c * 256 + t * P + P],
                                                       src[:, t, at + c * P:at + c * P + P], ident[:])
                    last.then_inc(mT_ready, 1)

            def mem_scores(l, t):
                pe.wait_ge(mT_taken, 2 * l + 2)
                pe.wait_ge(gained_ready, 16 if l == 0 else 32)
                for m in range(MH):
                    p0 = MD * (m % 2)
                    at = t * 1024 + MEM_AT[m] * 256
                    last = nc.tensor.matmul(flat[:, at:at + 256],
                                            mqT[p0:p0 + MD, m // 2, t * P:t * P + P],
                                            mkT[p0:p0 + MD, m // 2, :], start=True, stop=True)
                last.then_inc(ms_ready, 1)

            def mem_weights(l, groups=range(4)):
                for i in groups:
                    kt, c = i // 2, i % 2
                    if i == 0:
                        pe.wait_ge(mprob_ready, 2 * l + 2)
                    if i < 2:
                        pe.wait_ge(qkT_taken, 3 + i) if l == 0 else pe.wait_ge(fT_taken, 3 + i)
                    if i >= 2:
                        pe.wait_ge(mpT_taken, 4 * l + i - 1)
                    for m in range(2):
                        for t in range(T):
                            last = nc.tensor.transpose(tpb[i % 2][:, m * 256 + t * P:m * 256 + t * P + P],
                                                       mprob[:, t, 2 * c + m, kt * P:kt * P + P], ident[:])
                    last.then_inc(mpT_ready, 1)

            def mem_values(l):
                pe.wait_ge(mpT_taken, 4 * l + 4)
                for c in range(2):
                    for m in range(2):
                        for kt in range(2):
                            mh = 2 * c + m
                            last = nc.tensor.matmul(tpb[0][MD * m:MD * m + MD, c * 256:c * 256 + 256],
                                                    memkv_l[l][:, kt, 256 + MD * mh:256 + MD * mh + MD],
                                                    mprobT[:, kt, mh, :], start=(kt == 0), stop=(kt == 1))
                last.then_inc(mo_ready, 1)

            pe.wait_ge(ident_landed, 16)
            norm_transposes(0, (0,))
            pe.wait_ge(gains_landed, 64)
            nc.tensor.transpose(tpb[0][:, 0:72], gains_raw[:, :], ident[0:72, 0:72]).then_inc(gainsT_ready, 1)
            norm_transposes(0, (1,))
            ffn(0, 0)

            proj_unit(S_MK0, Y, 0, True, False, 1)
            norm_transposes(2)
            proj_unit(S_MK0 + 1, Y, 4, False, True, 1)

            def spans(n):
                if n == 0:
                    pe.wait_ge(loga_ready, 2)
                    pe.wait_ge(mexp_ready, 8)
                else:
                    pe.wait_ge(decay_ready, n)
                for hh in range(GH):
                    for t in range(T):
                        m = n + (t if n == NLEV - 1 else 0)
                        at = (hh * 2 + t) * P
                        last = nc.tensor.matmul(flat[0:DK, at:at + P], loga[:, t, hh * DK:hh * DK + DK],
                                                between[:, m * P:m * P + P], start=True, stop=True)
                last.then_inc(span_ready, 1)

            def level_scores(n):
                if n >= 1:
                    pe.wait_ge(joined_ready, n)
                    pe.wait_ge(score_taken, n)
                w = joined[(n - 1) % 2]
                if n == NLEV:
                    for hh in range(GH):
                        at = hh * 256
                        last = nc.tensor.matmul(flat[:, 1024 + hh * P:1024 + hh * P + P], w[:, at:at + P],
                                                w[:, at + P:at + 256], start=True, stop=True)
                else:
                    for i in range(GH * T):
                        lhs = kT if n == 0 else w
                        rhs = qT if n == 0 else w
                        last = nc.tensor.matmul(flat[:, 1024 + i * P:1024 + i * P + P], lhs[:, i * P:i * P + P],
                                                rhs[:, i * P:i * P + P], start=True, stop=True)
                last.then_inc(score_ready, 1)

            def head_transposes(w):
                for t in range(T):
                    pe.wait_ge(gneg_ready, 2) if w == 0 else pe.wait_ge(qkT_taken, t + 1)
                    for hh in range(GH):
                        at = w * 384 + hh * DK
                        last = nc.tensor.transpose(tpb[t][0:DK, hh * P:hh * P + P], qk[:, t, at:at + DK], ident[:])
                    last.then_inc(qkT_ready, 1)

            proj_unit(S_PA[0], X, 0, True, False, 2, bank_free=lambda t: chunk_free(1, t))
            norm_transposes(3)
            proj_unit(S_PA[0] + 1, X, 4, False, True, 2)
            proj_unit(S_PA[1], X, 0, True, False, 2, bank_free=lambda t: chunk_free(2, t))
            for t in range(T):
                last = nc.tensor.transpose(tpb[0][0:RANK, t * P:t * P + P], glow[:, t, :], ident[:])
            last.then_inc(glT_ready, 1)
            proj_unit(S_PA[1] + 1, X, 4, False, True, 2)
            pe.wait_ge(glT_taken, 1)
            mem_operands(0)
            proj_unit(S_PA[2], X, 0, True, False, 2, bank_free=lambda t: chunk_free(3, t))
            pe.wait_ge(const_landed, 16 * 9)
            pe.wait_ge(ones_set, 1)
            pe.wait_ge(mT_taken, 2)
            for t in range(T):
                nc.tensor.matmul(tpb[t][:, 0:GH * DK], glT[:, t * P:t * P + P], wgate,
                                 start=True, stop=False).then_inc(gate_product, 1)
                pe.wait_ge(gate_product, t + 1)
                nc.tensor.matmul(tpb[t][:, 0:GH * DK], ones_row, bgate,
                                 start=False, stop=True).then_inc(gate_ready, 1)
            mem_scores(0, 0)
            mem_scores(0, 1)
            proj_unit(S_PA[2] + 1, X, 4, False, True, 2)
            proj_unit(S_MK1, Y, 0, True, False, 3, bank_free=lambda t: chunk_free(4, t),
                      hooks={(0, 2): lambda: head_transposes(0), (1, 2): lambda: head_transposes(1)})
            proj_unit(S_MK1 + 1, Y, 4, False, True, 3,
                      hooks={(0, 2): lambda: mem_weights(0, (0, 1)), (1, 0): lambda: mem_weights(0, (2, 3))})
            mem_values(0)
            spans(0)

            def level_step(k):
                spans(k + 1)
                if k == 0:
                    pe.wait_ge(qkT_taken, 4)
                level_scores(k)

            proj_unit(S_PA[3], X, 0, True, False, 2, bank_free=lambda t: chunk_free(5, t),
                      hooks={(1, 0): lambda: level_step(0)})
            level_step(1)
            proj_unit(S_PA[3] + 1, X, 4, False, True, 2, hooks={(1, 0): lambda: level_step(2)})
            level_step(3)
            proj_unit(S_PA[4], X, 0, True, False, 2, bank_free=lambda t: chunk_free(6, t),
                      hooks={(1, 0): lambda: level_step(4)})
            level_step(5)
            proj_unit(S_PA[4] + 1, X, 4, False, True, 2, hooks={(1, 0): lambda: level_step(6)})
            level_scores(NLEV - 1)
            proj_unit(S_PA[5], X, 0, True, False, 2, bank_free=lambda t: chunk_free(7, t),
                      hooks={(1, 0): lambda: level_scores(NLEV)})
            for t in range(T):
                pe.wait_ge(score_taken, NLEV + t)
                for hh in range(GH):
                    dst = flat[:, gla_at(t, hh):gla_at(t, hh) + DV]
                    last = nc.tensor.matmul(dst, scores[:, (hh * 2 + t) * P:(hh * 2 + t + 1) * P],
                                            v_gla[:, t, hh * DV:hh * DV + DV], start=True, stop=(t == 0))
                    if t == 1:
                        last = nc.tensor.matmul(dst, cross[:, hh, :], v_gla[:, 0, hh * DV:hh * DV + DV],
                                                start=False, stop=True)
                last.then_inc(o_ready, 1)
            proj_unit(S_PA[5] + 1, X, 4, False, True, 2)

            def o_transposes(t):
                pe.wait_ge(ohead_ready, t + 1)
                for g in range(2):
                    pe.wait_ge(oTlo_ready, 2 * t - 1 + g) if t else pe.wait_ge(molo_ready, 1)
                    for k in range(4 if g == 0 else 2):
                        c = 4 * g + k
                        last = nc.tensor.transpose(tpb[g][:, k * P:k * P + P], ohead[:, t, c * P:c * P + P], ident[:])
                    last.then_inc(oT_ready, 1)

            out_hooks = [{(0, 0): lambda: o_transposes(0), (1, 0): lambda: o_transposes(1)},
                         {(0, 0): lambda: pe.wait_ge(oTlo_ready, 2), (1, 0): lambda: pe.wait_ge(oTlo_ready, 4)},
                         None, {(1, 1): lambda: norm_transposes(4, (0,))}]
            for u, k in enumerate(OUT_ORDER):
                out_unit(S_WO0 + u, *mixed(k), u == 0, u == 3,
                         hooks=out_hooks[u])
            ffn(1, 4)

            ffn(2, 5)

            def fox_transposes(steps):
                for n in steps:
                    i = FOX_T[n]
                    src = kv if i < 3 else qb
                    if n < 2:
                        pe.wait_ge(mT_taken, 4)
                    else:
                        pe.wait_ge(fT_taken, n - 1)
                    if n >= 4:
                        pe.wait_ge(cum_taken, 2)
                    for m in range(2):
                        for t in range(T):
                            hh = 2 * (i % 3) + m
                            last = nc.tensor.transpose(tpb[n % 2][:, m * 256 + t * P:m * 256 + t * P + P],
                                                       src[:, t, hh * FD:hh * FD + FD], ident[:])
                    last.then_inc(fT_ready, 1)

            def gate_sums():
                pe.wait_ge(fg_log, 1)
                pe.wait_ge(molo_ready, 2)
                logf = fg[:, 3]
                nc.tensor.matmul(tpb[0][0:FH, 0:256], logf[:, 0, :], upper[:], start=True, stop=False)
                nc.tensor.matmul(tpb[0][0:FH, P:256], logf[:, 1, :], upper[:, 0:P],
                                 start=False, stop=True).then_inc(cum_ready, 1)
                nc.tensor.matmul(tpb[1][:, 0:FH], upper[:, 0:P], logf[:, 0, :], start=True, stop=True)
                nc.tensor.matmul(tpb[1][:, 8:8 + FH], upper[:, P:256], logf[:, 0, :], start=True, stop=False)
                nc.tensor.matmul(tpb[1][:, 8:8 + FH], upper[:, 0:P], logf[:, 1, :],
                                 start=False, stop=True).then_inc(cum_ready, 1)

            def fox_scores(t):
                pe.wait_ge(fT_taken, 6)
                pe.wait_ge(mexp_ready, 16)
                wide = P * (t + 1)
                for hh in range(FH):
                    at = fox_at(t, hh)
                    nc.tensor.matmul(flat[:, at:at + wide], fqT[:, hh, t * P:t * P + P], fkT[:, hh, 0:wide],
                                     start=True, stop=False)
                    last = nc.tensor.matmul(flat[:, at:at + wide], pick[:, hh * P:hh * P + P], negD[:, 0:wide],
                                            start=False, stop=True)
                last.then_inc(fs_ready, 1)

            def weight_transposes(steps):
                for n in steps:
                    pe.wait_ge(fprob_ready, 1 if n < 2 else 2)
                    if n == 1:
                        pe.wait_ge(flogit_ready, 2)
                    if n >= 2:
                        pe.wait_ge(fpT_taken, n - 1)
                    if n < 2:
                        for m in range(4 if n == 0 else 2):
                            last = nc.tensor.transpose(tpb[n][:, m * P:m * P + P], fprob1[:, 4 * n + m, P:2 * P],
                                                       ident[:])
                    else:
                        for m in range(2):
                            for t in range(T):
                                p = (fprob0 if t == 0 else fprob1)[:, 2 * (n - 2) + m, 0:P]
                                last = nc.tensor.transpose(tpb[n % 2][:, m * 256 + t * P:m * 256 + t * P + P], p,
                                                           ident[:])
                    last.then_inc(fpT_ready, 1)

            def fox_values(c):
                pe.wait_ge(fpT_taken, c + 3)
                if c == 0:
                    chunk_free(14)
                for m in range(2):
                    hh = 2 * c + m
                    v0 = 768 + hh * FD
                    nc.tensor.matmul(fo_bank[c][:, m * 256:m * 256 + 256], kv[:, 0, v0:v0 + FD], fprobT0[:, hh, :],
                                     start=True, stop=False)
                    last = nc.tensor.matmul(fo_bank[c][:, m * 256 + P:m * 256 + 256], kv[:, 1, v0:v0 + FD],
                                            fprobT1[:, hh, :], start=False, stop=True)
                last.then_inc(fo_ready, 1)

            proj_unit(S_KV[0], Y, 0, True, False, 6)
            norm_transposes(7)
            proj_unit(S_KV[0] + 1, Y, 4, False, True, 6)
            proj_unit(S_PB[0], X, 0, True, False, 7, bank_free=lambda t: chunk_free(9, t))
            proj_unit(S_PB[0] + 1, X, 4, False, True, 7)
            proj_unit(S_KV[1], Y, 0, True, False, 6, bank_free=lambda t: chunk_free(10, t),
                      hooks={(1, 2): lambda: mem_operands(1)})
            mem_scores(1, 0)
            mem_scores(1, 1)
            proj_unit(S_KV[1] + 1, Y, 4, False, True, 6, hooks={(1, 0): lambda: fox_transposes((0, 1))})
            fox_transposes((2,))
            proj_unit(S_FG, Y, 0, True, True, 6, bank_free=lambda t: chunk_free(11, t),
                      hooks={(1, 0): lambda: fox_transposes((3,))})
            mem_weights(1, (0, 1))
            proj_unit(S_PB[1], X, 0, True, False, 7, bank_free=lambda t: chunk_free(12, t),
                      hooks={(1, 0): lambda: mem_weights(1, (2, 3))})
            mem_values(1)
            proj_unit(S_PB[1] + 1, X, 4, False, True, 7, hooks={(1, 0): lambda: gate_sums()})
            proj_unit(S_KV[2], Y, 0, True, False, 6, bank_free=lambda t: chunk_free(13, t),
                      hooks={(1, 0): lambda: fox_transposes((4, 5))})
            fox_scores(1)
            proj_unit(S_KV[2] + 1, Y, 4, False, True, 6, hooks={(1, 0): lambda: fox_scores(0)})
            out_hooks = {(0, 0): lambda: pe.wait_ge(flogit_ready, 1), (1, 0): lambda: weight_transposes((0, 1))}
            for u, k in enumerate(OUT_ORDER):
                if u > 0:
                    pe.wait_ge(folo_ready, u)
                if u == 3:
                    out_hooks = {(1, 1): lambda: norm_transposes(8, (0,))}
                out_unit(S_WO1 + u, *mixed(k), u == 0, u == 3, hooks=out_hooks)
                out_hooks = None
                if u == 0:
                    weight_transposes((2, 3))
                    fox_values(0)
                    weight_transposes((4,))
                    fox_values(1)
                    fox_values(2)
            ffn(3, 8)

        @block.scalar
        def _(act):
            following = [0]

            def split_hi(base, j=0, due=None):
                act.wait_ge(raw_landed[base % RING], due)
                if not isinstance(j, int) or base >= RING:
                    act.wait_ge(halves_done, 2 * (base + 3 * j - RING + 1))
                n = size(base) if isinstance(j, int) else 2048
                nc.scalar.copy(whi[base % RING][:, 0:n], raw[base % RING][:, 0:n]).then_inc(hi_ready, 1)

            def split(n):
                assert n == following[0]
                following[0] += 1
                if n < S_END:
                    split_hi(n, 0, landed(n))

            def split_next():
                if following[0] < S_END:
                    split(following[0])

            def norm_hi(s, tiles=range(T), groups=range(2)):
                xset = NORMS[s][2]
                for i in [4 * s + 2 * t + g for t in tiles for g in groups]:
                    t, g = (i % 4) // 2, i % 2
                    act.wait_ge(gained_ready, i + 1)
                    nc.scalar.copy(xhi[xset][:, 4 * g:4 * g + 4, t * P:t * P + P],
                                   gained[i % 2][:, :, :]).then_inc(xhi_ready, 1)

            def square_sums(st, rows_of, discard):
                for t in range(T):
                    if 2 * st + t:
                        act.wait_ge(squares_ready, 2 * st + t)
                    nc.scalar.activation(discard, rows_of[:, t, :], ACT.Square,
                                         accum_out=squares[:, st, t:t + 1]).then_inc(squares_ready, 1)

            def gate_hi(f, j):
                last_step = isinstance(j, int) and j == STEPS - 1
                dst = xhi[X][:, 0:2, :] if last_step else gthi[:, :, :]
                act.wait_ge(gT_ready, STEPS * f + j + 1)
                nc.scalar.copy(dst.rearrange("p c n -> p (c n)"), tpb[0]).then_inc(gthi_ready, 1)

            def tanh_in(f, st, base, j, tiles=range(T)):
                for t in tiles:
                    act.wait_ge(halves_done, 2 * base + 6 * j + t + 1)
                    nc.scalar.activation(th[:, t, :], inb[t][:, 0:256], ACT.Tanh,
                                         scale=rstd_half[:, st, t:t + 1]).then_inc(th_ready, 1)

            def ffn(f, st):
                B = S_FFN[f]
                assert following[0] == B + 2
                split_next()
                if f > 0:
                    norm_hi({1: 4, 2: 5, 3: 8}[f], (1,), (1,))
                act.wait_ge(stats_ready, st + 1)
                act.wait_ge(squares_ready, 2 * st + 2)
                if f == 0:
                    norm_hi(1, (0,))
                tanh_in(f, st, B + 1, 0, (0,))
                if f == 0:
                    norm_hi(1, (1,))
                if f == 2:
                    norm_hi(6, (0,))
                tanh_in(f, st, B + 1, 0, (1,))
                split_next()
                if f == 2:
                    norm_hi(6, (1,))
                gate_hi(f, 0)
                split_next()
                split_next()
                tanh_in(f, st, B + 3, 0)
                split_next()
                if f == 0:
                    square_sums(ST_MEM, mem, work[:, 4096:4096 + D])
                assert following[0] == B + 7
                with act.Fori(2, STEPS - 1) as j:
                    gate_hi(f, j - 1)
                    split_hi(B + 1, j, landed(B + 1 + 6) + 16 * (j - 2))
                    split_hi(B + 2, j, landed(B + 2 + 6) + 32 * (j - 2))
                    tanh_in(f, st, B, j)
                    split_hi(B + 3, j, landed(B + 3 + 6) + 32 * (j - 2))
                following[0] += 3 * (STEPS - 3)
                gate_hi(f, STEPS - 2)
                split_next()
                split_next()
                tanh_in(f, st, B + 3 * (STEPS - 1), 0)
                gate_hi(f, STEPS - 1)
                split_next()
                split_next()
                assert following[0] == B + FFN_UNITS + 2 or following[0] == S_END

            def take_chunk(n, pieces, st, tiles=range(T)):
                act.wait_ge(stats_ready, st + 1)
                for t in tiles:
                    act.wait_ge(halves_done, 2 * n + t + 1)
                    for dst, lo, hi in pieces:
                        last = nc.scalar.activation(dst[:, t, :], inb[t][:, lo:hi], ACT.Copy,
                                                    scale=rstd[:, st, t:t + 1])
                    last.then_inc(chunk_taken, 1)

            def mem_take(l):
                act.wait_ge(mT_ready, 2 * l + 1)
                nc.scalar.copy(mkT.rearrange("p a n -> p (a n)"), tpb[0]).then_inc(mT_taken, 1)
                act.wait_ge(mT_ready, 2 * l + 2)
                nc.scalar.mul(mqT.rearrange("p a n -> p (a n)"), tpb[1], MD ** -0.5).then_inc(mT_taken, 1)

            def mem_exp(l, t):
                act.wait_ge(mneg_ready, 2 * l + t + 1)
                for m in range(MH):
                    at = t * 1024 + MEM_AT[m] * 256
                    i = 4 * t + MEM_AT[m]
                    nc.scalar.activation(mprob[:, t, m, :], flat[:, at:at + 256], ACT.Exp,
                                         bias=mstat[:, 1, i:i + 1],
                                         accum_out=mstat[:, 2, i:i + 1]).then_inc(mexp_ready, 1)

            def mem_probT(l):
                for i in range(4):
                    act.wait_ge(mpT_ready, 4 * l + i + 1)
                    kt, c = i // 2, i % 2
                    nc.scalar.copy(mprobT[:, kt, 2 * c:2 * c + 2, :].rearrange("p h n -> p (h n)"),
                                   tpb[i % 2]).then_inc(mpT_taken, 1)

            def mem_out_hi(l):
                act.wait_ge(mo_ready, l + 1)
                nc.scalar.copy(gthi[:, :, :].rearrange("p c n -> p (c n)"), tpb[0]).then_inc(mohi_ready, 1)

            row = 0
            for name in ("norm_ffn", "norm_mix", "norm_mem", "norm_shared"):
                src = a[name]
                if len(src.shape) == 3:
                    src = src.rearrange("a b c -> (a b) c")
                if len(src.shape) == 2:
                    src = src.rearrange("a c -> (a c)")
                src = src.rearrange("(a c) -> a c", c=P)
                act.dma_start(gains_raw[row:row + src.shape[0], :], src).then_inc(gains_landed, 16)
                row += src.shape[0]
            split_next()
            norm_hi(0, (0,))
            split_next()
            norm_hi(0, (1,))
            square_sums(ST_X, h, scratch)
            ffn(0, ST_X)

            split_next()
            norm_hi(2)
            take_chunk(S_MK0 + 1, [(memkv_l[0], 0, 512)], ST_MEM, (0,))
            split_next()
            take_chunk(S_MK0 + 1, [(memkv_l[0], 0, 512)], ST_MEM, (1,))
            split_next()
            act.wait_ge(h_updated, 4)
            square_sums(ST_H, h, scratch)
            split_next()

            take_chunk(S_PA[0] + 1, [(glow, 0, 16), (qk[:, :, 768:1024], 16, 272)], ST_H)
            norm_hi(3)
            split_next()
            split_next()
            take_chunk(S_PA[1] + 1, [(qk[:, :, 0:512], 0, 512)], ST_H)
            split_next()
            mem_take(0)
            split_next()
            for t in range(T):
                act.wait_ge(gneg_ready, t + 1)
                nc.scalar.activation(gneg[:, t, :], gneg[:, t, :], ACT.Exp).then_inc(gexp_ready, 1)
            for t in range(T):
                act.wait_ge(gexp_ready, t + 1)
                nc.scalar.activation(gneg[:, t, :], gneg[:, t, :], ACT.Ln, bias=1.0).then_inc(gln_ready, 1)
            mem_exp(0, 0)
            mem_exp(0, 1)
            take_chunk(S_PA[2] + 1, [(qk[:, :, 512:768], 0, 256), (v_gla[:, :, 0:256], 256, 512)], ST_H)
            split_next()

            def head_take(i):
                w, t = i // 2, i % 2
                act.wait_ge(qkT_ready, i + 1)
                dst = (qT if w == 0 else kT).rearrange("p (h t n) -> p h t n", h=GH, t=T)[:, :, t, :]
                src = tpb[t][0:DK, :].rearrange("p (h n) -> p h n", h=GH)
                nc.scalar.mul(dst, src, DK ** -0.5 if w == 0 else 1.0).then_inc(qkT_taken, 1)

            def decays(n):
                act.wait_ge(span_ready, n + 1)
                if n >= 2:
                    act.wait_ge(joined_ready, n - 1)
                nc.scalar.activation(decay[n % 2], flat[0:DK, 0:1024], ACT.Exp).then_inc(decay_ready, 1)

            for i in range(4):
                head_take(i)
            split_next()
            mem_probT(0)
            take_chunk(S_MK1 + 1, [(memkv_l[1], 0, 512)], ST_MEM)
            mem_out_hi(0)
            decays(0)
            split_next()
            decays(1)
            decays(2)
            split_next()
            take_chunk(S_PA[3] + 1, [(v_gla[:, :, 256:768], 0, 512)], ST_H, (0,))
            decays(3)
            take_chunk(S_PA[3] + 1, [(v_gla[:, :, 256:768], 0, 512)], ST_H, (1,))
            decays(4)
            split_next()
            decays(5)
            decays(6)
            split_next()
            take_chunk(S_PA[4] + 1, [(r_gla[:, :, 0:384], 0, 384)], ST_H, (0,))
            decays(NLEV - 1)
            take_chunk(S_PA[4] + 1, [(r_gla[:, :, 0:384], 0, 384)], ST_H, (1,))
            split_next()

            def r_tanh(tiles, heads):
                act.wait_ge(chunk_taken, 14 if heads == 0 else 15 + tiles.start)
                cols = slice(2 * DV * heads, 2 * DV * heads + 2 * DV)
                nc.scalar.activation(sgate[:, tiles, cols], r_gla[:, tiles, cols], ACT.Tanh,
                                     scale=0.5).then_inc(rth_ready, 1)

            r_tanh(slice(0, T), 0)
            split_next()
            act.wait_ge(joined_ready, NLEV)
            for t in range(T):
                act.wait_ge(o_ready, t + 1)
                for hh in range(GH):
                    i = GH * t + hh
                    nc.scalar.activation(osquares[:, i * DV:i * DV + DV], flat[:, gla_at(t, hh):gla_at(t, hh) + DV],
                                         ACT.Square, accum_out=ostat[:, 0, i:i + 1]).then_inc(osq_ready, 1)
            for t in range(T):
                take_chunk(S_PA[5] + 1, [(r_gla[:, :, 384:768], 0, 384)], ST_H, (t,))
                r_tanh(slice(t, t + 1), 1)
            for i in range(4):
                if i == 2:
                    split_next()
                t, g = i // 2, i % 2
                k = 4 if g == 0 else 2
                act.wait_ge(oT_ready, i + 1)
                nc.scalar.copy(xhi[Y][:, 4 * g:4 * g + k, t * P:t * P + P],
                               tpb[g][:, 0:k * P].rearrange("p (k n) -> p k n", k=k)).then_inc(oThi_ready, 1)
            split_next()
            split_next()
            split_next()
            norm_hi(4, (0,))
            norm_hi(4, (1,), (0,))
            act.wait_ge(h_updated, 8)
            square_sums(ST_H + 1, h, scratch)
            ffn(1, ST_H + 1)

            norm_hi(5, (0,))
            norm_hi(5, (1,), (0,))
            act.wait_ge(h_updated, 12)
            square_sums(ST_H + 2, h, scratch)
            ffn(2, ST_H + 2)

            split_next()
            norm_hi(7)
            take_chunk(S_KV[0] + 1, [(kv[:, :, 0:512], 0, 512)], ST_H + 2, (0,))
            split_next()
            take_chunk(S_KV[0] + 1, [(kv[:, :, 0:512], 0, 512)], ST_H + 2, (1,))
            split_next()
            square_sums(ST_H + 3, h, scratch)
            split_next()
            take_chunk(S_PB[0] + 1, [(qb[:, :, 512:1024], 0, 512)], ST_H + 3)
            split_next()

            def fox_take(steps):
                for n in steps:
                    i = FOX_T[n]
                    act.wait_ge(fT_ready, n + 1)
                    dst = (fkT if i < 3 else fqT)[:, 2 * (i % 3):2 * (i % 3) + 2, :].rearrange("p h n -> p (h n)")
                    nc.scalar.mul(dst, tpb[n % 2], 1.0 if i < 3 else FD ** -0.5).then_inc(fT_taken, 1)

            def fox_exp(t):
                act.wait_ge(fneg_ready, 2 - t)
                p = fprob1 if t else fprob0
                for hh in range(FH):
                    i = FH * t + hh
                    nc.scalar.activation(p[:, hh, :], p[:, hh, :], ACT.Exp, bias=fstat[:, 1, i:i + 1],
                                         accum_out=fstat[:, 2, i:i + 1]).then_inc(fexp_ready, 1)

            mem_take(1)
            split_next()
            mem_exp(1, 0)
            fox_take((0, 1))
            mem_exp(1, 1)
            take_chunk(S_KV[1] + 1, [(kv[:, :, 512:1024], 0, 512)], ST_H + 2)
            fox_take((2,))
            split_next()
            fox_take((3,))
            split_next()
            act.wait_ge(fg_neg, 1)
            nc.scalar.activation(fg[:, 2], fg[:, 1], ACT.Exp).then_inc(fg_exp, 1)
            act.wait_ge(fg_exp, 1)
            nc.scalar.activation(fg[:, 1], fg[:, 2], ACT.Ln, bias=1.0).then_inc(fg_ln, 1)
            mem_probT(1)
            split_next()
            mem_out_hi(1)
            take_chunk(S_PB[1] + 1, [(qb[:, :, 0:512], 0, 512)], ST_H + 3)
            split_next()
            fox_take((4, 5))
            split_next()
            take_chunk(S_KV[2] + 1, [(kv[:, :, 1024:1536], 0, 512)], ST_H + 2, (0,))
            fox_exp(1)
            take_chunk(S_KV[2] + 1, [(kv[:, :, 1024:1536], 0, 512)], ST_H + 2, (1,))
            fox_exp(0)
            split_next()
            for n in range(5):
                act.wait_ge(fpT_ready, n + 1)
                if n == 0:
                    dst, src = fprobT1[:, 0:4, :], tpb[0]
                elif n == 1:
                    dst, src = fprobT1[:, 4:6, :], tpb[1][:, 0:256]
                else:
                    dst, src = fprobT0[:, 2 * (n - 2):2 * (n - 2) + 2, :], tpb[n % 2]
                nc.scalar.copy(dst.rearrange("p h n -> p (h n)"), src).then_inc(fpT_taken, 1)
            for c in range(3):
                act.wait_ge(fo_ready, c + 1)
                nc.scalar.copy(xhi[Y][:, 2 * c:2 * c + 2, :].rearrange("p c n -> p (c n)"),
                               fo_bank[c]).then_inc(fohi_ready, 1)
            split_next()
            split_next()
            split_next()
            norm_hi(8, (0,))
            norm_hi(8, (1,), (0,))
            act.wait_ge(h_updated, 20)
            square_sums(ST_H + 4, h, scratch)
            ffn(3, ST_H + 4)
            for t in range(T):
                act.wait_ge(h_updated, 20 + 2 * t + 2)
                act.wait_ge(squares_ready, 2 * (ST_H + 5) + t)
                nc.scalar.activation(work[:, D:2 * D], h[:, t, :], ACT.Square,
                                     accum_out=squares[:, ST_H + 5, t:t + 1]).then_inc(squares_ready, 1)

        @block.gpsimd
        def _(pool):
            nc.gpsimd.memset(power[:], -0.5).then_inc(power_set, 1)
            pool.wait_ge(power_set, 1)
            nc.gpsimd.memset(ones_row, 1.0).then_inc(ones_set, 1)
            pool.wait_ge(ones_set, 1)

            def row_stats(st):
                pool.wait_ge(squares_ready, 2 * st + 2)
                nc.gpsimd.tensor_scalar(meansq[:, st, :], squares[:, st, :], 1.0 / D, EPS, ALU.mult,
                                        ALU.add).then_inc(meansq_ready, 1)
                pool.wait_ge(meansq_ready, st + 1)
                nc.gpsimd.tensor_tensor(rstd[:, st, :], meansq[:, st, :], power[:, 0:T],
                                        ALU.pow).then_inc(rstd_ready, 1)
                pool.wait_ge(rstd_ready, st + 1)
                nc.gpsimd.tensor_scalar(rstd_half[:, st, :], rstd[:, st, :], 0.5, 0.0, ALU.mult,
                                        ALU.add).then_inc(half_ready, 1)
                pool.wait_ge(half_ready, st + 1)
                nc.gpsimd.tensor_tensor(rstd_sq_half[:, st, :], rstd[:, st, :], rstd_half[:, st, :],
                                        ALU.mult).then_inc(stats_ready, 1)

            row_stats(ST_X)
            row_stats(ST_MEM)
            pool.wait_ge(const_landed, 16 * 9)
            nc.gpsimd.tensor_copy(pair[:], pair_f32).then_inc(pair_ready, 1)
            row_stats(ST_H)
            pool.wait_ge(normT_ready, 16)
            pool.wait_ge(h_updated, 4)
            nc.gpsimd.memset(scores, 0.0).then_inc(scores_zero, 1)
            for t in range(T):
                cols = slice(GH * t, GH * t + GH)
                pool.wait_ge(osq_ready, GH * (t + 1))
                nc.gpsimd.tensor_scalar(ostat[:, 1, cols], ostat[:, 0, cols], 1.0 / DV, EPS, ALU.mult,
                                        ALU.add).then_inc(omean_ready, 1)
                pool.wait_ge(omean_ready, t + 1)
                nc.gpsimd.tensor_tensor(ostat[:, 2, cols], ostat[:, 1, cols], power[:, 0:GH],
                                        ALU.pow).then_inc(orstd_ready, 1)
            for st in range(ST_H + 1, ST_H + 5):
                row_stats(st)
            st = ST_H + 5
            for t in range(T):
                pool.wait_ge(squares_ready, 2 * st + t + 1)
                nc.gpsimd.tensor_scalar(meansq[:, st, t:t + 1], squares[:, st, t:t + 1], 1.0 / D, EPS, ALU.mult,
                                        ALU.add).then_inc(meansq_ready, 1)
                pool.wait_ge(meansq_ready, st + t + 1)
                nc.gpsimd.tensor_tensor(rstd[:, st, t:t + 1], meansq[:, st, t:t + 1], power[:, 0:1],
                                        ALU.pow).then_inc(rstd_ready, 1)

        @block.vector
        def _(dve):
            following = [0]

            def split_lo(base, j=0):
                dve.wait_ge(hi_ready, base + 3 * j + 1)
                n = size(base) if isinstance(j, int) else 2048
                r = base % RING
                nc.vector.tensor_tensor(wlo[r][:, 0:n], raw[r][:, 0:n], whi[r][:, 0:n].bitcast(F32),
                                        ALU.subtract).then_inc(lo_ready, 1)

            def split_next():
                if following[0] < S_END:
                    split_lo(following[0])
                    following[0] += 1

            def norm_gain(i):
                s, t, g = i // 4, (i % 4) // 2, i % 2
                row = NORMS[s][1]
                dve.wait_ge(normT_ready, i + 1 if s < 6 else i - 3)
                if i >= 2:
                    dve.wait_ge(xlo_ready, i - 1)
                nc.vector.tensor_tensor(
                    gained[i % 2][:, :, :], acc[2 * t + g].rearrange("p (k n) -> p k n", k=4),
                    gains[:, 8 * row + 4 * g:8 * row + 4 * g + 4].unsqueeze(2).to_broadcast([P, 4, P]),
                    ALU.mult).then_inc(gained_ready, 1)

            def norm_lo(i):
                s, t, g = i // 4, (i % 4) // 2, i % 2
                xset = NORMS[s][2]
                dve.wait_ge(xhi_ready, i + 1)
                nc.vector.tensor_tensor(xlo[xset][:, 4 * g:4 * g + 4, t * P:t * P + P], gained[i % 2][:, :, :],
                                        xhi[xset][:, 4 * g:4 * g + 4, t * P:t * P + P].bitcast(F32),
                                        ALU.subtract).then_inc(xlo_ready, 1)

            def norm_tile(s, t):
                for i in (4 * s + 2 * t, 4 * s + 2 * t + 1):
                    norm_gain(i)
                for i in (4 * s + 2 * t, 4 * s + 2 * t + 1):
                    norm_lo(i)

            def norm(s, split_between=False):
                norm_gain(4 * s)
                norm_gain(4 * s + 1)
                norm_lo(4 * s)
                norm_gain(4 * s + 2)
                norm_lo(4 * s + 1)
                if split_between:
                    split_next()
                norm_gain(4 * s + 3)
                norm_lo(4 * s + 2)
                norm_lo(4 * s + 3)

            def update_h(n, scale, tiles=range(T)):
                for t in tiles:
                    dve.wait_ge(halves_done, 2 * n + t + 1)
                    for c in range(2):
                        nc.vector.scalar_tensor_tensor(
                            out=h[:, t, 512 * c:512 * c + 512], in0=acc[2 * t + c], scalar=scale,
                            in1=h[:, t, 512 * c:512 * c + 512], op0=ALU.mult, op1=ALU.add).then_inc(h_updated, 1)

            def update_and_norm(n, scale, s):
                update_h(n, scale, (0,))
                norm_gain(4 * s)
                norm_gain(4 * s + 1)
                norm_lo(4 * s)
                update_h(n, scale, (1,))
                norm_gain(4 * s + 2)
                norm_lo(4 * s + 1)
                norm_lo(4 * s + 2)
                split_next()
                norm_gain(4 * s + 3)
                norm_lo(4 * s + 3)

            def gate_lo(f, j):
                last_step = isinstance(j, int) and j == STEPS - 1
                hi, lo = (x[:, 0:2, :] for x in ((xhi[X], xlo[X]) if last_step else (gthi, gtlo)))
                dve.wait_ge(gthi_ready, STEPS * f + j + 1)
                nc.vector.tensor_tensor(lo.rearrange("p c n -> p (c n)"), tpb[0],
                                        hi.bitcast(F32).rearrange("p c n -> p (c n)"),
                                        ALU.subtract).then_inc(gtlo_ready, 1)

            def gate(f, st, j, tiles=range(T)):
                for t in tiles:
                    i = 2 * STEPS * f + t + 1
                    dve.wait_ge(th_ready, i + 2 * j)
                    nc.vector.scalar_tensor_tensor(out=half[:, t, :], in0=th[:, t, :], scalar=1.0,
                                                   in1=inb[t][:, 0:256], op0=ALU.add,
                                                   op1=ALU.mult).then_inc(y_ready, 1)
                    dve.wait_ge(y_ready, i + 2 * j)
                    nc.vector.scalar_tensor_tensor(out=gated[:, t, :], in0=inb[t][:, 256:512],
                                                   scalar=rstd_sq_half[:, st, t:t + 1], in1=half[:, t, :],
                                                   op0=ALU.mult, op1=ALU.mult).then_inc(g_ready, 1)

            def ffn(f, st):
                B = S_FFN[f]
                assert following[0] == B + 2
                split_next()
                dve.wait_ge(stats_ready, st + 1)
                if f == 0:
                    norm_tile(1, 0)
                gate(f, st, 0, (0,))
                if f == 0:
                    norm_tile(1, 1)
                if f == 2:
                    norm_tile(6, 0)
                gate(f, st, 0, (1,))
                split_next()
                if f == 2:
                    norm_tile(6, 1)
                gate_lo(f, 0)
                split_next()
                split_next()
                gate(f, st, 1)
                split_next()
                with dve.Fori(2, STEPS - 1) as j:
                    gate_lo(f, j - 1)
                    split_lo(B + 1, j)
                    split_lo(B + 2, j)
                    gate(f, st, j)
                    split_lo(B + 3, j)
                following[0] += 3 * (STEPS - 3)
                gate_lo(f, STEPS - 2)
                split_next()
                split_next()
                gate(f, st, STEPS - 1)
                gate_lo(f, STEPS - 1)
                split_next()

            def mem_max(l, t):
                dve.wait_ge(ms_ready, 2 * l + t + 1)
                i = 4 * t
                nc.vector.tensor_reduce(mstat[:, 0, i:i + 4],
                                        flat[:, t * 1024:t * 1024 + 1024].rearrange("p (h n) -> p h n", h=4),
                                        AX_X, ALU.max).then_inc(mmax_ready, 1)
                dve.wait_ge(mmax_ready, 2 * l + t + 1)
                nc.vector.tensor_scalar(mstat[:, 1, i:i + 4], mstat[:, 0, i:i + 4], -1.0, None,
                                        ALU.mult).then_inc(mneg_ready, 1)

            def mem_norm(l, t):
                i = 4 * t
                dve.wait_ge(mexp_ready, 8 * l + 4 * t + 4)
                nc.vector.reciprocal(mstat[:, 3, i:i + 4], mstat[:, 2, i:i + 4]).then_inc(mrecip_ready, 1)
                dve.wait_ge(mrecip_ready, 2 * l + t + 1)
                for m in range(MH):
                    last = nc.vector.tensor_scalar(mprob[:, t, m, :], mprob[:, t, m, :],
                                                   mstat[:, 3, i + MEM_AT[m]:i + MEM_AT[m] + 1], None,
                                                   ALU.mult)
                last.then_inc(mprob_ready, 1)

            def mem_out_lo(l):
                dve.wait_ge(mohi_ready, l + 1)
                nc.vector.tensor_tensor(gtlo[:, :, :].rearrange("p c n -> p (c n)"), tpb[0],
                                        gthi[:, :, :].bitcast(F32).rearrange("p c n -> p (c n)"),
                                        ALU.subtract).then_inc(molo_ready, 1)

            dve.wait_ge(gainsT_ready, 1)
            nc.vector.tensor_copy(gains[:], tpb[0][:, 0:72]).then_inc(gains_ready, 1)
            dve.wait_ge(gains_ready, 1)
            norm_gain(0)
            norm_gain(1)
            split_next()
            norm_lo(0)
            norm_lo(1)
            norm_gain(2)
            norm_gain(3)
            norm_lo(2)
            norm_lo(3)
            split_next()
            ffn(0, ST_X)

            update_h(S_FFN0 + FFN_UNITS - 1, 0.5)
            split_next()
            norm(2, True)
            split_next()
            split_next()
            split_next()
            norm(3)
            split_next()
            dve.wait_ge(glT_ready, 1)
            dve.wait_ge(pair_ready, 1)
            nc.vector.tensor_copy(glT, tpb[0][0:RANK, 0:256]).then_inc(glT_taken, 1)
            split_next()
            split_next()
            split_next()
            for t in range(T):
                dve.wait_ge(gate_ready, t + 1)
                nc.vector.tensor_scalar(gmin[:, t, :], tpb[t][:, 0:GH * DK], 0.0, None,
                                        ALU.min).then_inc(gmin_ready, 1)
                dve.wait_ge(gmin_ready, t + 1)
                nc.vector.scalar_tensor_tensor(out=gneg[:, t, :], in0=gmin[:, t, :], scalar=2.0,
                                               in1=tpb[t][:, 0:GH * DK], op0=ALU.mult,
                                               op1=ALU.subtract).then_inc(gneg_ready, 1)
            mem_max(0, 0)
            mem_max(0, 1)
            for t in range(T):
                dve.wait_ge(gln_ready, t + 1)
                nc.vector.tensor_tensor(loga[:, t, :], gmin[:, t, :], gneg[:, t, :],
                                        ALU.subtract).then_inc(loga_ready, 1)
            mem_norm(0, 0)
            mem_norm(0, 1)
            split_next()
            split_next()
            mem_out_lo(0)

            def take_scores(n):
                dve.wait_ge(score_ready, n + 1)
                if n == NLEV:
                    nc.vector.tensor_copy(cross[:, :, :].rearrange("p h n -> p (h n)"),
                                          flat[:, 1024:1536]).then_inc(score_taken, 1)
                    return
                if n:
                    dve.wait_ge(score_taken, n)
                nc.vector.copy_predicated(
                    scores.rearrange("p (i n) -> p i n", n=P),
                    pair[:, n * P:n * P + P].unsqueeze(1).to_broadcast([P, GH * T, P]),
                    flat[:, 1024:2048].rearrange("p (i n) -> p i n", n=P)).then_inc(score_taken, 1)

            def join(n):
                b = 1 << n
                dve.wait_ge(decay_ready, n + 1)
                if n >= 2:
                    dve.wait_ge(score_ready, n)
                for s, src in ((0, kT), (1, qT)):
                    pick_half = lambda ap: ap.rearrange("p (m s b) -> p m s b", s=2, b=b)[:, :, s, :]
                    last = nc.vector.tensor_tensor(pick_half(joined[n % 2][:, :]), pick_half(decay[n % 2]),
                                                   pick_half(src), ALU.mult)
                last.then_inc(joined_ready, 1)

            dve.wait_ge(scores_zero, 1)
            dve.wait_ge(qkT_taken, 4)
            join(0)
            split_next()
            for n in range(NLEV):
                if n >= 1:
                    join(n)
                if n < NLEV - 1:
                    take_scores(n)
                if n in (1, 3, 5):
                    split_next()
            take_scores(NLEV - 1)
            split_next()
            take_scores(NLEV)

            def r_silu(tiles, heads, i):
                cols = slice(2 * DV * heads, 2 * DV * heads + 2 * DV)
                dve.wait_ge(rth_ready, i + 1)
                nc.vector.scalar_tensor_tensor(out=sgate[:, tiles, cols], in0=sgate[:, tiles, cols], scalar=1.0,
                                               in1=r_gla[:, tiles, cols], op0=ALU.add,
                                               op1=ALU.mult).then_inc(rsilu_ready, 1)
                dve.wait_ge(rsilu_ready, i + 1)
                for t in range(tiles.start, tiles.stop):
                    v = sgate[:, t, cols].rearrange("p (h n) -> p h n", h=2)
                    last = nc.vector.scalar_tensor_tensor(
                        out=v, in0=v, scalar=0.5, in1=ghead[:, :].unsqueeze(1).to_broadcast([P, 2, DV]),
                        op0=ALU.mult, op1=ALU.mult)
                last.then_inc(sgate_ready, 1)

            def gate_heads(t, heads):
                for hh in heads:
                    at = gla_at(t, hh)
                    last = nc.vector.scalar_tensor_tensor(
                        out=ohead[:, t, hh * DV:hh * DV + DV], in0=flat[:, at:at + DV],
                        scalar=ostat[:, 2, GH * t + hh:GH * t + hh + 1],
                        in1=sgate[:, t, hh * DV:hh * DV + DV], op0=ALU.mult, op1=ALU.mult)
                return last

            r_silu(slice(0, T), 0, 0)
            split_next()
            dve.wait_ge(sgate_ready, 1)
            for t in range(T):
                dve.wait_ge(orstd_ready, t + 1)
                gate_heads(t, (0, 1))
            for t in range(T):
                r_silu(slice(t, t + 1), 1, t + 1)
                dve.wait_ge(sgate_ready, t + 2)
                gate_heads(t, (2, 3)).then_inc(ohead_ready, 1)
            for i in range(4):
                if i == 2:
                    split_next()
                t, g = i // 2, i % 2
                k = 4 if g == 0 else 2
                dve.wait_ge(oThi_ready, i + 1)
                nc.vector.tensor_tensor(xlo[Y][:, 4 * g:4 * g + k, t * P:t * P + P],
                                        tpb[g][:, 0:k * P].rearrange("p (k n) -> p k n", k=k),
                                        xhi[Y][:, 4 * g:4 * g + k, t * P:t * P + P].bitcast(F32),
                                        ALU.subtract).then_inc(oTlo_ready, 1)
            split_next()
            split_next()
            update_and_norm(S_WO0 + 3, 1.0, 4)
            ffn(1, ST_H + 1)

            update_and_norm(S_FFN1 + FFN_UNITS - 1, 0.5, 5)
            ffn(2, ST_H + 2)

            update_h(S_FFN2 + FFN_UNITS - 1, 0.5)
            split_next()
            split_next()
            norm(7)
            for _ in range(4):
                split_next()
            mem_max(1, 0)
            mem_max(1, 1)
            split_next()
            mem_norm(1, 0)
            mem_norm(1, 1)
            split_next()
            for t in range(T):
                dve.wait_ge(halves_done, 2 * S_FG + t + 1)
                nc.vector.scalar_tensor_tensor(out=fg[:, 0, t, :], in0=inb[t][:, 0:FH],
                                               scalar=rstd[:, ST_H + 2, t:t + 1], in1=bf[:], op0=ALU.mult,
                                               op1=ALU.add).then_inc(fg_logit, 1)
                dve.wait_ge(fg_logit, t + 1)
                nc.vector.tensor_scalar(fg[:, 3, t, :], fg[:, 0, t, :], 0.0, None, ALU.min).then_inc(chunk_taken, 1)
            dve.wait_ge(chunk_taken, 24)
            nc.vector.scalar_tensor_tensor(out=fg[:, 1], in0=fg[:, 3], scalar=2.0, in1=fg[:, 0], op0=ALU.mult,
                                           op1=ALU.subtract).then_inc(fg_neg, 1)
            split_next()
            dve.wait_ge(fg_ln, 1)
            nc.vector.tensor_tensor(fg[:, 3], fg[:, 3], fg[:, 1], ALU.subtract).then_inc(fg_log, 1)
            split_next()
            mem_out_lo(1)
            dve.wait_ge(cum_ready, 1)
            nc.vector.tensor_scalar(negD[:], tpb[0][0:FH, 0:256], -1.0, None, ALU.mult).then_inc(cum_taken, 1)
            dve.wait_ge(cum_ready, 2)
            nc.vector.tensor_copy(Dtok[:, :, :], tpb[1][:, 0:16].rearrange("p (t n) -> p t n", t=2)[:, :, 0:FH]
                                  ).then_inc(cum_taken, 1)
            dve.wait_ge(cum_taken, 2)
            split_next()
            split_next()
            for n, t in enumerate((1, 0)):
                dve.wait_ge(fs_ready, n + 1)
                p = fprob1 if t else fprob0
                wide = P * (t + 1)
                mask = causal[:, :] if t else causal[:, P:2 * P]
                for hh in range(FH):
                    at = fox_at(t, hh)
                    last = nc.vector.scalar_tensor_tensor(out=p[:, hh, :], in0=flat[:, at:at + wide],
                                                          scalar=Dtok[:, t, hh:hh + 1], in1=mask, op0=ALU.add,
                                                          op1=ALU.add)
                last.then_inc(flogit_ready, 1)
                dve.wait_ge(flogit_ready, n + 1)
                i = FH * t
                nc.vector.tensor_reduce(fstat[:, 0, i:i + FH], p[:, :, :], AX_X, ALU.max).then_inc(fmax_ready, 1)
                dve.wait_ge(fmax_ready, n + 1)
                nc.vector.tensor_scalar(fstat[:, 1, i:i + FH], fstat[:, 0, i:i + FH], -1.0, None,
                                        ALU.mult).then_inc(fneg_ready, 1)
            for n, t in enumerate((1, 0)):
                dve.wait_ge(fexp_ready, FH * (n + 1))
                p = fprob1 if t else fprob0
                i = FH * t
                nc.vector.reciprocal(fstat[:, 3, i:i + FH], fstat[:, 2, i:i + FH]).then_inc(frecip_ready, 1)
                dve.wait_ge(frecip_ready, n + 1)
                for hh in range(FH):
                    last = nc.vector.tensor_scalar(p[:, hh, :], p[:, hh, :], fstat[:, 3, i + hh:i + hh + 1], None,
                                                   ALU.mult)
                last.then_inc(fprob_ready, 1)
            split_next()
            for c in range(3):
                dve.wait_ge(fohi_ready, c + 1)
                nc.vector.tensor_tensor(xlo[Y][:, 2 * c:2 * c + 2, :].rearrange("p c n -> p (c n)"), fo_bank[c],
                                        xhi[Y][:, 2 * c:2 * c + 2, :].bitcast(F32).rearrange("p c n -> p (c n)"),
                                        ALU.subtract).then_inc(folo_ready, 1)
            split_next()
            split_next()
            update_and_norm(S_WO1 + 3, 1.0, 8)
            ffn(3, ST_H + 4)

            dve.wait_ge(final_landed, 16)
            for t in range(T):
                update_h(S_FFN3 + FFN_UNITS - 1, 0.5, (t,))
                dve.wait_ge(rstd_ready, ST_H + 5 + t + 1)
                for c in range(2):
                    cols = slice(512 * c, 512 * c + 512)
                    nc.vector.scalar_tensor_tensor(out=h[:, t, cols], in0=h[:, t, cols],
                                                   scalar=rstd[:, ST_H + 5, t:t + 1], in1=gfinal[:, cols],
                                                   op0=ALU.mult, op1=ALU.mult).then_inc(out_ready, 1)


def gla_at(t, h):
    return (2 * t + h // 2) * 512 + (h % 2) * DV


def fox_at(t, h):
    if t == 1:
        return h * 256
    return 3 * 512 + h * P if h < 4 else 7 * 512 + (h - 4) * P


H_UPDATES_BEFORE = {2: 1, 4: 2, 5: 3, 7: 4, 8: 5}


_INS = ["x", "mem", "norm_ffn", "w_ffn_in", "w_ffn_out", "norm_mix", "norm_mem", "w_mem_kv", "w_out", "w_in_a",
        "w_gate_up", "b_gate", "norm_gla_head", "w_in_b", "norm_shared", "w_kv_shared", "w_fgate", "b_fgate",
        "norm_final"]


def kernel(**inputs):
    import concourse.bacc as _bacc
    from concourse.bass_utils import run_bass_kernel_spmd as _run

    nc = _bacc.Bacc("TRN2", target_bir_lowering=False, num_devices=1)
    arrays, args = {}, {}
    host = {n: np.ascontiguousarray(inputs[n]) for n in _INS}
    host.update(shape_constants())
    for name, v in host.items():
        arrays[f"in_{name}_dram"] = v
        args[name] = nc.dram_tensor(f"in_{name}_dram", v.shape, mybir.dt.from_np(v.dtype),
                                    kind="ExternalInput").ap()
    out = nc.dram_tensor("out_0_dram", (1, T * P, D), F32, kind="ExternalOutput").ap()
    build(nc, args, out)
    r = _run(nc, [arrays], core_ids=[0])
    return r.results[0]["out_0_dram"]
```
